# Optimizing a Trainium2 kernel written in Bass

```python
import jax, jax.numpy as jnp
from jax import lax
import numpy as np

D_MODEL = 1024
BATCH = 1
SEQ = 512
DEPTH = 2

CHUNK = 64
Q_BLOCK = 128
EPS = 1e-6
NEG_INF = -1e30

MLA_HEADS = 8
QK_NOPE = 64
QK_ROPE = 32
V_HEAD = 64
Q_LORA = 256
KV_LORA = 128
ROPE_THETA = 10000.0
MLA_WIDTH = MLA_HEADS * V_HEAD

POOL_WINDOWS = (2, 4, 8, 16)
POOL_GROUPS = 4
POOL_GROUP_DIM = 64
POOL_WIDTH = POOL_GROUPS * POOL_GROUP_DIM
POOL_MAX_WIN = 16

SGU_BLOCK = 128
SGU_GROUPS = 4
SGU_GROUP_DIM = 64
SGU_WIDTH = SGU_GROUPS * SGU_GROUP_DIM

CONV_K = 3
CONV_WIDTH = 256

N_BRANCH = 4
D_FF = ((8 * D_MODEL + 3 * 256 - 1) // (3 * 256)) * 256

IN_SIZES = (Q_LORA, KV_LORA, QK_ROPE, POOL_WIDTH, SGU_WIDTH, SGU_WIDTH,
            CONV_WIDTH, CONV_WIDTH, CONV_WIDTH, N_BRANCH * D_MODEL)
IN_WIDTH = sum(IN_SIZES)


def rmsnorm(x, g):
    xf = x.astype(jnp.float32)
    y = xf * lax.rsqrt(jnp.mean(xf * xf, axis=-1, keepdims=True) + EPS)
    return (y * g.astype(jnp.float32)).astype(x.dtype)

def split_cols(p):
    out = []
    o = 0
    for n in IN_SIZES:
        out.append(p[..., o:o + n])
        o += n
    return out

def rope_tables(seq, dtype):
    inv = ROPE_THETA ** (-jnp.arange(0, QK_ROPE, 2, dtype=jnp.float32) / QK_ROPE)
    ang = jnp.arange(seq, dtype=jnp.float32)[:, None] * inv[None, :]
    return jnp.cos(ang).astype(dtype), jnp.sin(ang).astype(dtype)

def apply_rope(x, cos, sin):
    half = x.shape[-1] // 2
    x1, x2 = x[..., :half], x[..., half:]
    return jnp.concatenate([x1 * cos - x2 * sin, x2 * cos + x1 * sin], axis=-1)

def mla_branch(c_q, c_kv, k_r, g_cq, g_ckv, w_uq, w_ukv, cos, sin):
    B, S, _ = c_q.shape
    q = (rmsnorm(c_q, g_cq) @ w_uq).reshape(B, S, MLA_HEADS, QK_NOPE + QK_ROPE)
    q_nope = q[..., :QK_NOPE]
    q_rope = apply_rope(q[..., QK_NOPE:], cos[:, None, :], sin[:, None, :])
    kv = (rmsnorm(c_kv, g_ckv) @ w_ukv).reshape(B, S, MLA_HEADS, QK_NOPE + V_HEAD)
    k_nope, v = kv[..., :QK_NOPE], kv[..., QK_NOPE:]
    k_rope = apply_rope(k_r, cos, sin)
    scale = (QK_NOPE + QK_ROPE) ** -0.5
    chunk_id = jnp.arange(S) // CHUNK
    outs = []
    for blk in range(S // Q_BLOCK):
        q0 = blk * Q_BLOCK
        kend = q0 + Q_BLOCK
        s = (jnp.einsum('bqhd,bkhd->bhqk', q_nope[:, q0:kend], k_nope[:, :kend])
             + jnp.einsum('bqhr,bkr->bhqk', q_rope[:, q0:kend], k_rope[:, :kend]))
        s = s.astype(jnp.float32) * scale
        mask = chunk_id[q0:kend, None] >= chunk_id[None, :kend]
        s = jnp.where(mask[None, None], s, NEG_INF)
        p = jax.nn.softmax(s, axis=-1).astype(v.dtype)
        outs.append(jnp.einsum('bhqk,bkhd->bqhd', p, v[:, :kend]))
    return jnp.concatenate(outs, axis=1).reshape(B, S, MLA_WIDTH)

def pool_branch(z, w_grp, scale):
    B, S, _ = z.shape
    zg = z.reshape(B, S, POOL_GROUPS, POOL_GROUP_DIM).astype(jnp.float32)
    csp = jnp.pad(jnp.cumsum(zg, axis=1), ((0, 0), (POOL_MAX_WIN, 0), (0, 0), (0, 0)))
    t = jnp.arange(S)
    outs = []
    for g, w in enumerate(POOL_WINDOWS):
        win_sum = (csp[:, POOL_MAX_WIN:POOL_MAX_WIN + S, g]
                   - csp[:, POOL_MAX_WIN - w:POOL_MAX_WIN - w + S, g])
        count = jnp.minimum(t + 1, w).astype(jnp.float32)
        outs.append(win_sum / count[None, :, None] - zg[:, :, g])
    pooled = jnp.stack(outs, axis=2).astype(z.dtype)
    mixed = jnp.einsum('bsgc,gcd->bsgd', pooled, w_grp)
    return mixed.reshape(B, S, POOL_WIDTH) * scale

def sgu_branch(u, v, g_v, w_s, b_s):
    B, S, _ = u.shape
    n = S // SGU_BLOCK
    vn = rmsnorm(v, g_v).reshape(B, n, SGU_BLOCK, SGU_GROUPS, SGU_GROUP_DIM)
    pos_chunk = jnp.arange(SGU_BLOCK) // CHUNK
    mask = pos_chunk[:, None] >= pos_chunk[None, :]
    w = jnp.where(mask[None], w_s, 0)
    mixed = jnp.einsum('gij,bnjgc->bnigc', w, vn) + b_s.T[None, None, :, :, None]
    return u * mixed.reshape(B, S, SGU_WIDTH)

def conv_branch(b_gate, c_gate, x_in, w_conv):
    z = c_gate * x_in
    y = lax.conv_general_dilated(z, w_conv, window_strides=(1,),
                                 padding=[(CONV_K - 1, 0)],
                                 dimension_numbers=('NWC', 'WIO', 'NWC'),
                                 feature_group_count=CONV_WIDTH)
    return b_gate * y

def first_inputs(seed: int = 0) -> dict:
    key = jax.random.key(seed)
    ks = iter(jax.random.split(key, 32))

    def nrm(shape, fan_in):
        return jax.random.normal(next(ks), shape, jnp.float32) * (fan_in ** -0.5)

    def gain(shape):
        return 1.0 + 0.1 * jax.random.normal(next(ks), shape, jnp.float32)

    L = DEPTH
    return {
        "x": jax.random.normal(next(ks), (BATCH, SEQ, D_MODEL), jnp.float32),
        "w_in": nrm((L, D_MODEL, IN_WIDTH), D_MODEL),
        "g_pre_mix": gain((L, D_MODEL)),
        "g_cq": gain((L, Q_LORA)),
        "g_ckv": gain((L, KV_LORA)),
        "w_uq": nrm((L, Q_LORA, MLA_HEADS * (QK_NOPE + QK_ROPE)), Q_LORA),
        "w_ukv": nrm((L, KV_LORA, MLA_HEADS * (QK_NOPE + V_HEAD)), KV_LORA),
        "pool_w": nrm((L, POOL_GROUPS, POOL_GROUP_DIM, POOL_GROUP_DIM), POOL_GROUP_DIM),
        "pool_scale": gain((L, POOL_WIDTH)),
        "g_sgu_v": gain((L, SGU_WIDTH)),
        "sgu_w": nrm((L, SGU_GROUPS, SGU_BLOCK, SGU_BLOCK), SGU_BLOCK),
        "sgu_b": gain((L, SGU_GROUPS, SGU_BLOCK)),
        "conv_w": nrm((L, CONV_K, 1, CONV_WIDTH), CONV_K),
        "w_br_a": nrm((L, MLA_WIDTH, D_MODEL), MLA_WIDTH),
        "w_br_b": nrm((L, POOL_WIDTH, D_MODEL), POOL_WIDTH),
        "w_br_c": nrm((L, SGU_WIDTH, D_MODEL), SGU_WIDTH),
        "w_br_d": nrm((L, CONV_WIDTH, D_MODEL), CONV_WIDTH),
        "w_out": nrm((L, D_MODEL, D_MODEL), D_MODEL),
        "g_post_mix": gain((L, D_MODEL)),
        "g_pre_ffn": gain((L, D_MODEL)),
        "w_ffn_gate": nrm((L, D_MODEL, D_FF), D_MODEL),
        "w_ffn_up": nrm((L, D_MODEL, D_FF), D_MODEL),
        "w_ffn_down": nrm((L, D_FF, D_MODEL), D_FF),
        "g_post_ffn": gain((L, D_MODEL)),
    }

def first_block(x, w_in, g_pre_mix, g_cq, g_ckv, w_uq, w_ukv, pool_w, pool_scale,
              g_sgu_v, sgu_w, sgu_b, conv_w, w_br_a, w_br_b, w_br_c, w_br_d,
              w_out, g_post_mix, g_pre_ffn, w_ffn_gate, w_ffn_up, w_ffn_down,
              g_post_ffn):
    B, S, D = x.shape
    cos, sin = rope_tables(S, x.dtype)
    for l in range(DEPTH):
        h = rmsnorm(x, g_pre_mix[l])
        (c_q, c_kv, k_r, p_in, s_u, s_v, cv_b, cv_c, cv_x,
         gate_logits) = split_cols(h @ w_in[l])
        y_a = mla_branch(c_q, c_kv, k_r, g_cq[l], g_ckv[l], w_uq[l], w_ukv[l], cos, sin) @ w_br_a[l]
        y_b = pool_branch(p_in, pool_w[l], pool_scale[l]) @ w_br_b[l]
        y_c = sgu_branch(s_u, s_v, g_sgu_v[l], sgu_w[l], sgu_b[l]) @ w_br_c[l]
        y_d = conv_branch(cv_b, cv_c, cv_x, conv_w[l]) @ w_br_d[l]
        gates = jax.nn.sigmoid(gate_logits.astype(jnp.float32)).astype(x.dtype)
        gates = gates.reshape(B, S, N_BRANCH, D)
        merged = (gates[:, :, 0] * y_a + gates[:, :, 1] * y_b
                  + gates[:, :, 2] * y_c + gates[:, :, 3] * y_d)
        x = x + rmsnorm(merged @ w_out[l], g_post_mix[l])
        h = rmsnorm(x, g_pre_ffn[l])
        f = (jax.nn.silu(h @ w_ffn_gate[l]) * (h @ w_ffn_up[l])) @ w_ffn_down[l]
        x = x + rmsnorm(f, g_post_ffn[l])
    return x


N_A = DEPTH // 2
N_B = DEPTH - N_A
LEFT_CHUNKS = 8
BAND = (LEFT_CHUNKS + 1) * CHUNK
PAD = LEFT_CHUNKS * CHUNK
D_RNN = D_MODEL
LRU_BLOCKS = 8
LRU_BW = D_RNN // LRU_BLOCKS
CONV_W = 4
LRU_C = 8.0
N_HEADS = 16
HEAD_DIM = D_MODEL // N_HEADS
MAX_REL = 2 * CHUNK
MIN_REL = -(CHUNK - 1)
NREL = MAX_REL - MIN_REL + 1
D_FF_2 = 4 * D_MODEL


def rmsnorm_2(x, g):
    xf = x.astype(jnp.float32)
    y = xf * lax.rsqrt(jnp.mean(xf * xf, axis=-1, keepdims=True) + EPS)
    return (y * g.astype(jnp.float32)).astype(x.dtype)

def causal_depthwise_conv(x, w, b):
    s = x.shape[1]
    xp = jnp.pad(x, ((0, 0), (CONV_W - 1, 0), (0, 0)))
    out = b + xp[:, 0:s] * w[0]
    for k in range(1, CONV_W):
        out = out + xp[:, k:k + s] * w[k]
    return out

def rg_lru(x, w_gate, b_gate, lam):
    bsz, s, _ = x.shape
    xf = x.astype(jnp.float32)
    xb = xf.reshape(bsz, s, LRU_BLOCKS, LRU_BW)
    g = jnp.einsum('bsnd,nde->bsne', xb, w_gate.astype(jnp.float32)) + b_gate.astype(jnp.float32)
    r = jax.nn.sigmoid(g[..., :LRU_BW]).reshape(bsz, s, D_RNN)
    i = jax.nn.sigmoid(g[..., LRU_BW:]).reshape(bsz, s, D_RNN)
    log_a = -LRU_C * r * jax.nn.softplus(-lam.astype(jnp.float32))
    a = jnp.exp(log_a)
    b = jnp.sqrt(-jnp.expm1(2.0 * log_a)) * (i * xf)

    def combine(left, right):
        a1, b1 = left
        a2, b2 = right
        return a1 * a2, a2 * b1 + b2

    _, h = lax.associative_scan(combine, (a, b), axis=1)
    return h.astype(x.dtype)

def recurrent_block(x, w_in, conv_w, conv_b, w_gate, b_gate, lam, w_out):
    u = x @ w_in
    gate, rec = u[..., :D_RNN], u[..., D_RNN:]
    rec = causal_depthwise_conv(rec, conv_w, conv_b)
    h = rg_lru(rec, w_gate, b_gate, lam)
    return (jax.nn.gelu(gate) * h) @ w_out

def shared_kv(x, kv_norm, w_kv, k_norm):
    bsz, s, _ = x.shape
    h = rmsnorm_2(x, kv_norm)
    kv = (h @ w_kv).reshape(bsz, s, 2, N_HEADS, HEAD_DIM)
    k = rmsnorm_2(kv[:, :, 0], k_norm)
    v = kv[:, :, 1]
    k = jnp.pad(k.transpose(0, 2, 1, 3), ((0, 0), (0, 0), (PAD, 0), (0, 0)))
    v = jnp.pad(v.transpose(0, 2, 1, 3), ((0, 0), (0, 0), (PAD, 0), (0, 0)))
    return k, v

def chunk_band_attention(q, k_pad, v_pad, rel_bias):
    bsz, s = q.shape[:2]
    nc = s // CHUNK
    qc = q.reshape(bsz, nc, CHUNK, N_HEADS, HEAD_DIM).transpose(1, 0, 3, 2, 4)
    qi = jnp.arange(CHUNK)[:, None]
    kj = jnp.arange(BAND)[None, :]
    dist = qi + PAD - kj
    idx = jnp.clip(dist, MIN_REL, MAX_REL) - MIN_REL
    bias = rel_bias.astype(jnp.float32)[:, idx]
    scale = HEAD_DIM ** -0.5

    def one_chunk(args):
        c, qb = args
        kb = lax.dynamic_slice_in_dim(k_pad, c * CHUNK, BAND, axis=2)
        vb = lax.dynamic_slice_in_dim(v_pad, c * CHUNK, BAND, axis=2)
        sc = jnp.einsum('bhqd,bhkd->bhqk', qb, kb).astype(jnp.float32) * scale + bias
        valid = (c * CHUNK - PAD + jnp.arange(BAND)) >= 0
        sc = jnp.where(valid, sc, -jnp.inf)
        p = jax.nn.softmax(sc, axis=-1).astype(vb.dtype)
        return jnp.einsum('bhqk,bhkd->bhqd', p, vb)

    o = lax.map(one_chunk, (jnp.arange(nc), qc))
    return o.transpose(1, 0, 3, 2, 4).reshape(bsz, s, N_HEADS * HEAD_DIM)

def sqrelu_mlp(x, w_up, w_down):
    return jnp.square(jax.nn.relu(x @ w_up)) @ w_down

def second_inputs(seed: int = 0) -> dict:
    key = jax.random.key(seed)
    ks = jax.random.split(key, 24)
    f32 = jnp.float32

    def nrm(k, shape, fan_in):
        return jax.random.normal(k, shape, f32) * (fan_in ** -0.5)

    def gain(k, shape):
        return 1.0 + 0.05 * jax.random.normal(k, shape, f32)

    x = jax.random.normal(ks[0], (BATCH, SEQ, D_MODEL), f32)
    a_norm = gain(ks[1], (N_A, D_MODEL))
    a_w_in = nrm(ks[2], (N_A, D_MODEL, 2 * D_RNN), D_MODEL)
    a_conv_w = nrm(ks[3], (N_A, CONV_W, D_RNN), CONV_W)
    a_conv_b = 0.01 * jax.random.normal(ks[4], (N_A, D_RNN), f32)
    a_w_gate = nrm(ks[5], (N_A, LRU_BLOCKS, LRU_BW, 2 * LRU_BW), LRU_BW)
    a_b_gate = 0.01 * jax.random.normal(ks[6], (N_A, LRU_BLOCKS, 2 * LRU_BW), f32)
    u = jax.random.uniform(ks[7], (N_A, D_RNN), f32, 0.9, 0.999)
    base = u ** (1.0 / LRU_C)
    a_lambda = jnp.log(base) - jnp.log1p(-base)
    a_w_out = nrm(ks[8], (N_A, D_RNN, D_MODEL), D_RNN)
    kv_norm = gain(ks[9], (D_MODEL,))
    w_kv = nrm(ks[10], (D_MODEL, 2 * N_HEADS * HEAD_DIM), D_MODEL)
    k_norm = gain(ks[11], (HEAD_DIM,))
    b_norm = gain(ks[12], (N_B, D_MODEL))
    b_w_q = nrm(ks[13], (N_B, D_MODEL, N_HEADS * HEAD_DIM), D_MODEL)
    b_q_norm = gain(ks[14], (N_B, HEAD_DIM))
    b_rel_bias = 0.1 * jax.random.normal(ks[15], (N_B, N_HEADS, NREL), f32)
    b_w_o = nrm(ks[16], (N_B, N_HEADS * HEAD_DIM, D_MODEL), N_HEADS * HEAD_DIM)
    mlp_norm = gain(ks[17], (DEPTH, D_MODEL))
    w_up = nrm(ks[18], (DEPTH, D_MODEL, D_FF_2), D_MODEL)
    w_down = nrm(ks[19], (DEPTH, D_FF_2, D_MODEL), D_FF_2)
    return {'x': x, 'a_norm': a_norm, 'a_w_in': a_w_in, 'a_conv_w': a_conv_w,
            'a_conv_b': a_conv_b, 'a_w_gate': a_w_gate, 'a_b_gate': a_b_gate,
            'a_lambda': a_lambda, 'a_w_out': a_w_out, 'kv_norm': kv_norm, 'w_kv': w_kv,
            'k_norm': k_norm, 'b_norm': b_norm, 'b_w_q': b_w_q, 'b_q_norm': b_q_norm,
            'b_rel_bias': b_rel_bias, 'b_w_o': b_w_o, 'mlp_norm': mlp_norm,
            'w_up': w_up, 'w_down': w_down}

def second_block(x, a_norm, a_w_in, a_conv_w, a_conv_b, a_w_gate, a_b_gate, a_lambda,
              a_w_out, kv_norm, w_kv, k_norm, b_norm, b_w_q, b_q_norm, b_rel_bias,
              b_w_o, mlp_norm, w_up, w_down):
    bsz, s, _ = x.shape
    h = x
    k_pad = None
    v_pad = None
    for l in range(DEPTH):
        if l < N_A:
            h = h + recurrent_block(rmsnorm_2(h, a_norm[l]), a_w_in[l], a_conv_w[l], a_conv_b[l],
                                    a_w_gate[l], a_b_gate[l], a_lambda[l], a_w_out[l])
        else:
            if l == N_A:
                k_pad, v_pad = shared_kv(h, kv_norm, w_kv, k_norm)
            j = l - N_A
            q = (rmsnorm_2(h, b_norm[j]) @ b_w_q[j]).reshape(bsz, s, N_HEADS, HEAD_DIM)
            q = rmsnorm_2(q, b_q_norm[j])
            o = chunk_band_attention(q, k_pad, v_pad, b_rel_bias[j])
            h = h + o @ b_w_o[j]
        h = h + sqrelu_mlp(rmsnorm_2(h, mlp_norm[l]), w_up[l], w_down[l])
    return h


def setup_inputs(seed=0):
    out = dict(first_inputs(seed))
    for name, value in second_inputs(seed + 1).items():
        if name != "x":
            out[name + "_2"] = value
    return out


def reference(
    x, w_in, g_pre_mix, g_cq, g_ckv, w_uq, w_ukv, pool_w, pool_scale, g_sgu_v, sgu_w, sgu_b,
    conv_w, w_br_a, w_br_b, w_br_c, w_br_d, w_out, g_post_mix, g_pre_ffn, w_ffn_gate, w_ffn_up,
    w_ffn_down, g_post_ffn, a_norm_2, a_w_in_2, a_conv_w_2, a_conv_b_2, a_w_gate_2, a_b_gate_2,
    a_lambda_2, a_w_out_2, kv_norm_2, w_kv_2, k_norm_2, b_norm_2, b_w_q_2, b_q_norm_2,
    b_rel_bias_2, b_w_o_2, mlp_norm_2, w_up_2, w_down_2,
):
    x = first_block(
        x, w_in, g_pre_mix, g_cq, g_ckv, w_uq, w_ukv, pool_w, pool_scale, g_sgu_v, sgu_w, sgu_b,
        conv_w, w_br_a, w_br_b, w_br_c, w_br_d, w_out, g_post_mix, g_pre_ffn, w_ffn_gate,
        w_ffn_up, w_ffn_down, g_post_ffn,
    )
    return second_block(
        x, a_norm_2, a_w_in_2, a_conv_w_2, a_conv_b_2, a_w_gate_2, a_b_gate_2, a_lambda_2,
        a_w_out_2, kv_norm_2, w_kv_2, k_norm_2, b_norm_2, b_w_q_2, b_q_norm_2, b_rel_bias_2,
        b_w_o_2, mlp_norm_2, w_up_2, w_down_2,
    )


_drawn_inputs = setup_inputs


def setup_inputs(seed=0):
    import zlib

    import numpy as np

    out = dict(_drawn_inputs(seed))
    spreads = {}
    factors = {'g_cq': 6.738,
     'g_ckv': 4.102,
     'a_norm_2': 4.298,
     'a_conv_b_2': 3.94,
     'a_b_gate_2': 8.0,
     'kv_norm_2': 8.0,
     'k_norm_2': 8.0,
     'b_norm_2': 8.0,
     'b_q_norm_2': 8.0,
     'b_rel_bias_2': 8.0}
    for name, (base, spread) in spreads.items():
        noise = np.random.default_rng([zlib.crc32(name.encode()), seed]).standard_normal(out[name].shape)
        drawn = base * np.exp(spread * noise) if base else spread * noise
        out[name] = __import__('jax').numpy.asarray(drawn.astype(out[name].dtype))
    for name, factor in factors.items():
        out[name] = (out[name] * factor).astype(out[name].dtype)
    return out
```

```python
import concourse.bass as bass
from concourse import mybir
from contextlib import ExitStack

F32 = mybir.dt.float32
F32R = mybir.dt.float32r
ALU = mybir.AluOpType
ACT = mybir.ActivationFunctionType
AX = mybir.AxisListType

P = 128
S = 512
D = 1024
DT = D // P
EPS = 1e-6
NEG = -1e30
UNIT = 8 * P
WSLOTS = 4
RSLOTS = 2
AHEAD = 3

L1 = 2
H1, NOPE, ROPE, VH = 8, 64, 32, 64
QK = NOPE + ROPE
FT = 22
CHUNKS = (8, 8, 6)
U_IN, U_QKV, U_MERGE, U_OUT = 16, 3, 6 * DT, DT
U_FFN = 2 * FT + DT * len(CHUNKS)
U_LAYER = U_IN + U_QKV + U_MERGE + U_OUT + U_FFN
H2, HD2 = 16, 64
QUARTERS = 4
U_AIN, U_AGATE, U_AOUT = 16, 2, DT
U_MLP = QUARTERS * 2 * DT
U_K, U_V, U_Q, U_O = DT, 8, DT, DT
U_SECOND = U_AIN + U_AGATE + U_AOUT + U_MLP + U_K + U_V + U_Q + U_O + U_MLP
NU = L1 * U_LAYER + U_SECOND
B2 = L1 * U_LAYER

_names = []
for _l in range(L1):
    _names += [(f"pre_mix{_l}", 8), (f"cq{_l}", 2), (f"ckv{_l}", 1), (f"pool_scale{_l}", 2), (f"conv{_l}", 6),
               (f"post_mix{_l}", 8), (f"pre_ffn{_l}", 8), (f"post_ffn{_l}", 8)]
_names += [("a_norm", 8), ("a_conv", 32), ("a_conv_b", 8), ("a_bg", 16), ("a_lam", 8), ("kv_norm", 8),
           ("k_norm", 1), ("b_norm", 8), ("q_norm", 1), ("mlp0", 8), ("mlp1", 8), ("inv_win", 2), ("eps", 1)]
VCOL, NV = {}, 0
for _n, _k in _names:
    VCOL[_n] = NV
    NV += _k

NORMS = {}
_base = 0
for _l in range(L1):
    for _n, _t in ((f"pre_mix{_l}", 8), (f"cq{_l}", 2), (f"ckv{_l}", 1), (f"post_mix{_l}", 8), (f"pre_ffn{_l}", 8),
                   (f"post_ffn{_l}", 8)):
        NORMS[_n] = (len(NORMS), _base, _t)
        _base += _t
for _n in ("a_norm", "mlp0", "kv_norm", "mlp1"):
    NORMS[_n] = (len(NORMS), _base, 8)
    _base += 8
def _split_plan():
    at, plan = 0, {}
    def add(name, n):
        nonlocal at
        plan[name] = at
        at += n
    for l in range(L1):
        add(f"pre_mix{l}", 8), add(f"cq{l}", 2), add(f"ckv{l}", 1), add(f"pool{l}", 2), add(f"sgu{l}", 2)
        add(f"conv{l}", 2), add(f"att{l}", H1), add(f"pre_ffn{l}", 8), add(f"ffn{l}", FT)
    add("a_norm", 8), add("rec", 8), add("lru", 8), add("mlp_in0", 8), add("mlp0", 32)
    add("kv_norm", 8), add("b_norm", 8), add("att2", H2), add("mlp_in1", 8), add("mlp1", 32)
    return plan
SPLIT = _split_plan()
SRC, _gap = {}, 0
for _n, _at in SPLIT.items():
    SRC[_n] = _at - _gap
    _gap += {"pool": 2, "att": H1}.get(_n[:-1], 0) if _n != "att2" else H2
XDONE = {"post_mix0": 0, "post_ffn0": 8, "post_mix1": 16, "post_ffn1": 24, "a_out": 32, "mlp0": 40, "b_out": 48, "mlp1": 56}


def build(nc, xT, w_all, vecs, cossin, win_fix, pool_w, sgu_wT, sgu_b, sgu_g, bias2, outT):
    base = (nc.sbuf_base + 31) // 32 * 32
    place = [base]

    def at(name, shape, dt, offset):
        return nc.alloc_sbuf_tensor_at(name, shape, dt, offset=offset)

    def room(nbytes):
        o = place[0]
        place[0] += (nbytes + 31) // 32 * 32
        assert place[0] <= nc.sbuf_usable_end, place[0]
        return o
    KB = 1024
    X = at("X", [P, DT, S], F32, room(16 * KB))
    w_raw = at("w_raw", [P, RSLOTS, UNIT], F32, room(RSLOTS * 4 * KB))
    w_hi = at("w_hi", [P, WSLOTS, UNIT], F32R, room(WSLOTS * 4 * KB))
    w_lo = at("w_lo", [P, WSLOTS, UNIT], F32R, room(WSLOTS * 4 * KB))
    oh = room(32 * KB)
    H_hi = at("H_hi", [P, DT, S], F32R, oh)
    H_lo = at("H_lo", [P, DT, S], F32R, oh + 16 * KB)
    lru_r = at("lru_r", [P, DT, S], F32, oh)
    lru_i = at("lru_i", [P, DT, S], F32, oh + 16 * KB)
    rel_bias = at("rel_bias", [P, H2, 2 * P], F32, oh)
    o1 = room(32 * KB)
    A = at("A", [P, 16, S], F32, o1)
    Q1 = at("Q1", [P, DT, S], F32, o1)
    K1 = at("K1", [P, DT, S], F32, o1 + 16 * KB)
    M_hi = at("M_hi", [P, DT, S], F32R, o1)
    M_lo = at("M_lo", [P, DT, S], F32R, o1 + 16 * KB)
    gelu_g = at("gelu_g", [P, DT, S], F32, o1)
    rec = at("rec", [P, DT, S], F32, o1 + 16 * KB)
    oy = room(40 * KB)
    Y_hi = at("Y_hi", [P, 10, S], F32R, oy)
    Y_lo = at("Y_lo", [P, 10, S], F32R, oy + 20 * KB)
    o3 = room(25 * KB)
    V1 = at("V1", [P, 4, S], F32, o3)
    probs = at("probs", [P, 2, 1280], F32, o3 + 8 * KB)
    probsT = at("probsT", [P, 1280], F32, o3 + 18 * KB)
    C_hi = at("C_hi", [P, 3, S], F32R, o3)
    C_lo = at("C_lo", [P, 3, S], F32R, o3 + 6 * KB)
    Z = at("Z", [P, 2, 528], F32, o3 + 12 * KB)
    ZW = 4224
    SA = at("SA", [P, 2, 528], F32, o3 + 12 * KB + ZW)
    SB = at("SB", [P, 2, 528], F32, o3 + 12 * KB + 2 * ZW)
    gates = at("gates", [P, 4, S], F32, o3)
    ysb = at("ysb", [P, 4, S], F32, o3 + 8 * KB)
    tmp = at("tmp", [P, 2, S], F32, o3 + 16 * KB)
    Dn = at("Dn", [P, DT, S], F32, o3)
    recp = at("recp", [P, DT, 520], F32, o3)
    lru_t = at("lru_t", [P, DT, S], F32, o3)
    lru_u = at("lru_u", [P, S], F32, o3 + 20 * KB)
    fa = at("fa", [P, 2, S], F32, o3 + 16 * KB)
    fb = at("fb", [P, 2, S], F32, o3 + 20 * KB)
    V2 = at("V2", [P, 4, D], F32, o3)
    probs2 = at("probs2", [P, 2, 1280], F32, oh + 16 * KB)
    probsT2 = at("probsT2", [P, 1280], F32, oh + 26 * KB)
    RS = at("RS", [P, S], F32, room(2 * KB))
    ACC = at("ACC", [P, S], F32, room(2 * KB))
    SQ = at("SQ", [P, 2, S], F32, room(4 * KB))
    XS = at("XS", [P, 2, S], F32, room(4 * KB))
    V = at("V", [P, NV], F32, room(NV * 4))
    CS = at("CS", [P, S], F32, room(2 * KB))
    ident = at("ident", [P, P], F32, room(512))
    ones = at("ones", [P, P], F32, room(512))
    ones64 = at("ones64", [P, P], F32, room(512))
    sel_row = at("sel_row", [1, P], F32, room(512))
    neg_row = at("neg_row", [1, P], F32, room(512))
    winfix = at("winfix", [P, 2, 16], F32, room(128))
    poolw = at("poolw", [P, 2, 64], F32, room(512))
    sguw = at("sguw", [P, 4, P], F32, room(2 * KB))
    sgub = at("sgub", [P, 2, P], F32, room(KB))
    sgug = at("sgug", [P, 256], F32, room(KB))
    st = at("st", [P, 2, 16], F32, room(128))
    sp = at("sp", [P, 40], F32, room(160))
    vnT = at("vnT", [P, 4, 256], F32, o3 + 12 * KB)

    ctx = ExitStack()
    with ctx:
        ps = ctx.enter_context(nc.psum_tensor("ps", [P, 8, S], F32))

        def sem(n):
            return ctx.enter_context(nc.semaphore(n))
        w_loaded = [sem(f"w_loaded{i}") for i in range(RSLOTS)]
        w_hi_ready, w_lo_ready, w_used, unit_out = sem("w_hi_ready"), sem("w_lo_ready"), sem("w_used"), sem("unit_out")
        x_loaded, consts_loaded, consts_made = sem("x_loaded"), sem("consts_loaded"), sem("consts_made")
        layer_loaded = sem("layer_loaded")
        x_done = sem("x_done")
        sq_ready, sq_added, ssum_ready, std_ready = sem("sq_ready"), sem("sq_added"), sem("ssum_ready"), sem("std_ready")
        src_ready = sem("src_ready")
        hi_ready = sem("hi_ready")
        lo_ready = sem("lo_ready")
        chain = sem("chain")
        a_chain = sem("a_chain")
        kr_ready, kr_spread = sem("kr_ready"), sem("kr_spread")
        qk_mm, qk_out = sem("qk_mm"), sem("qk_out")
        br_mm, br_act, br_vec = sem("br_mm"), sem("br_act"), sem("br_vec")
        s_ready, max_ready, exp_done, s_free = sem("s_ready"), sem("max_ready"), sem("exp_done"), sem("s_free")
        p_ready, t_done, pt_a, pt_v, pv_done = sem("p_ready"), sem("t_done"), sem("pt_a"), sem("pt_v"), sem("pv_done")
        sig_done, merged_lo = sem("sig_done"), sem("merged_lo")
        f_lin, f_act, f_src = sem("f_lin"), sem("f_act"), sem("f_src")
        lru_act, lru_vec = sem("lru_act"), sem("lru_vec")
        hn_sq, hn_mm, hn_std, hn_done = sem("hn_sq"), sem("hn_mm"), sem("hn_std"), sem("hn_done")
        bias_loaded = sem("bias_loaded")
        stored = sem("stored")

        def v(name, k=0, n=1):
            return V[:, VCOL[name] + k:VCOL[name] + k + n]

        def f(ap):
            return ap.bitcast(F32)

        def first_units(l):
            u = l * U_LAYER
            return dict(win=u, qkv=u + U_IN, merge=u + U_IN + U_QKV, out=u + U_IN + U_QKV + U_MERGE,
                        ffn=u + U_IN + U_QKV + U_MERGE + U_OUT)

        UG = B2 + U_AIN
        UAO = UG + U_AGATE
        UM0 = UAO + U_AOUT
        UK = UM0 + U_MLP
        UVV = UK + U_K
        UQ = UVV + U_V
        UO = UQ + U_Q
        UM1 = UO + U_O

        block = ctx.enter_context(nc.Block())

        @block.sync
        def _(eng):
            eng.dma_start(V[:], vecs).then_inc(consts_loaded, 16)
            for k in range(DT):
                eng.dma_start(X[:, k, :], xT[k * P:(k + 1) * P, :]).then_inc(x_loaded, 16)
            for s in range(RSLOTS):
                eng.dma_start(w_raw[:, s, :], w_all[s]).then_inc(w_loaded[s], 16)
            eng.dma_start(CS[:], cossin).then_inc(consts_loaded, 16)
            eng.dma_start(winfix[:], win_fix).then_inc(consts_loaded, 16)
            with eng.Fori(1, NU // RSLOTS) as i:
                for s in range(RSLOTS):
                    eng.wait_ge(w_lo_ready, i * RSLOTS + (s - RSLOTS + 1))
                    eng.dma_start(w_raw[:, s, :], w_all[bass.ds(i * RSLOTS + s, 1)].rearrange("o p n -> (o p) n")).then_inc(w_loaded[s], 16)
            for k in range(DT):
                eng.wait_ge(x_done, XDONE["mlp1"] + k + 1)
                eng.dma_start(outT[k * P:(k + 1) * P, :], X[:, k, :]).then_inc(stored, 16)
            eng.wait_ge(stored, 16 * DT)

        @block.gpsimd
        def _(eng):
            made = [0]

            def make(ins):
                made[0] += 1
                ins.then_inc(consts_made, 1)
                eng.wait_ge(consts_made, made[0])
            make(eng.memset(ident[:], 0.0))
            make(eng.affine_select(out=ident[:], in_=ident[:], compare_op=ALU.not_equal, fill=1.0, base=0,
                                   pattern=[[-1, P]], channel_multiplier=1))
            make(eng.memset(ones[:], 1.0))
            make(eng.memset(ones64[:], 0.0))
            make(eng.memset(ones64[0:64, 0:64], 1.0))
            make(eng.memset(ones64[64:128, 64:128], 1.0))
            make(eng.memset(sel_row[:], 0.0))
            make(eng.memset(sel_row[0:1, 0:64], 1.0))
            make(eng.memset(neg_row[:], 0.0))
            make(eng.memset(neg_row[0:1, 64:128], NEG))
            for l in range(L1):
                if l:
                    eng.wait_ge(lo_ready, SPLIT[f"conv{l - 1}"] + 2)
                    eng.wait_ge(layer_loaded, 64 * l)
                eng.dma_start(poolw[:], pool_w[l]).then_inc(layer_loaded, 16)
                eng.dma_start(sguw[:], sgu_wT[l]).then_inc(layer_loaded, 16)
                eng.dma_start(sgub[:], sgu_b[l]).then_inc(layer_loaded, 16)
                eng.dma_start(sgug[:], sgu_g[l]).then_inc(layer_loaded, 16)
                lo, n = (0, U_LAYER // 2 // WSLOTS) if l == 0 else (U_LAYER // 2 // WSLOTS, NU // WSLOTS)
                with eng.Fori(lo, n) as i:
                    for s in range(WSLOTS):
                        eng.wait_ge(w_hi_ready, i * WSLOTS + (s + 1))
                        nc.gpsimd.tensor_tensor(w_lo[:, s, :], w_raw[:, s % RSLOTS, :], f(w_hi[:, s, :]),
                                                ALU.subtract).then_inc(w_lo_ready, 1)

        @block.scalar
        def _(act):
            def split_weights(u, c):
                if isinstance(u, int) and u >= NU:
                    return
                act.wait_ge(w_loaded[c % RSLOTS], (u - (c % RSLOTS)) * (16 // RSLOTS) + 16)
                if not isinstance(u, int) or u >= WSLOTS:
                    act.wait_ge(w_used, u + (1 - WSLOTS))
                nc.scalar.activation(w_hi[:, c % WSLOTS, :], w_raw[:, c % RSLOTS, :], ACT.Copy).then_inc(w_hi_ready, 1)

            def tick(u, c=None):
                split_weights(u + AHEAD, (u if c is None else c) + AHEAD)

            def norm(name, src, ready, d, first=None):
                n, b, t = NORMS[name]
                for k in range(t):
                    act.wait_ge(ready[0], ready[1] + (ready[2] if len(ready) > 2 else 1) * (k + 1))
                    if b + k >= 2:
                        act.wait_ge(sq_added, b + k - 1)
                    nc.scalar.activation(SQ[:, (b + k) % 2, :], src(k), ACT.Square).then_inc(sq_ready, 1)
                act.wait_ge(ssum_ready, n + 1)
                act.wait_ge(sq_added, b + t)
                nc.scalar.activation(SQ[:, (b + t) % 2, :], ps[:, 7, :], ACT.Sqrt, bias=v("eps"), scale=1.0 / d).then_inc(std_ready, 1)

            def split_src(name, t, dst, src):
                for k in range(t):
                    act.wait_ge(src_ready, SRC[name] + k + 1)
                    nc.scalar.activation(dst(k), src(k), ACT.Copy).then_inc(hi_ready, 1)

            def xs(name):
                return lambda k: XS[:, k % 2, :]

            def attention(g0, heads, split, second):
                def exps(g):
                    h = g - g0
                    act.wait_ge(max_ready, g + 1)
                    if g >= 2 and not second:
                        act.wait_ge(t_done, g - 1)
                    off = 0
                    for j in range(4):
                        w = P * (j + 1)
                        o = (probs2 if second else probs)[:, g % 2, off:off + w]
                        if second:
                            i = nc.scalar.activation(o, o, ACT.Exp, bias=st[:, g % 2, j:j + 1], scale=1.0, accum_out=st[:, g % 2, 4 + j:5 + j])
                        else:
                            i = nc.scalar.activation(o, ps[:, j, 0:w], ACT.Exp, bias=st[:, g % 2, j:j + 1],
                                                     scale=QK ** -0.5, accum_out=st[:, g % 2, 4 + j:5 + j])
                        off += w
                    i.then_inc(exp_done, 1)
                exps(g0)
                for g in range(g0, g0 + heads):
                    h = g - g0
                    if h + 1 < heads:
                        exps(g + 1)
                    act.wait_ge(t_done, g + 1)
                    if g:
                        act.wait_ge(pv_done, g)
                    nc.scalar.activation((probsT2 if second else probsT)[:, 0:S], ps[:, 4, :], ACT.Copy).then_inc(pt_a, 1)
                    r = slice(64 * (h % 2), 64 * (h % 2) + 64)
                    act.wait_ge(pv_done, g + 1)
                    nc.scalar.activation(Y_hi[r, h // 2, :], ps[r, 7, :], ACT.Copy).then_inc(hi_ready, 1)

            act.wait_ge(consts_loaded, 48)
            for u in range(AHEAD):
                split_weights(u, u)
            for l in range(L1):
                U = first_units(l)
                if l == 0:
                    norm("pre_mix0", lambda k: X[:, k, :], (x_loaded, 16 * DT, 0), D)
                else:
                    norm(f"pre_mix{l}", lambda k: X[:, k, :], (x_done, XDONE[f"post_ffn{l - 1}"]), D)
                split_src(f"pre_mix{l}", 8, lambda k: H_hi[:, k, :], xs(0))
                for u in range(U["win"], U["win"] + U_IN):
                    tick(u)
                norm(f"cq{l}", lambda k: A[:, k, :], (unit_out, U["win"]), 256)
                split_src(f"cq{l}", 2, lambda k: C_hi[:, k, :], xs(0))
                norm(f"ckv{l}", lambda k: A[:, 2 + k, :], (unit_out, U["win"] + 2), 128)
                split_src(f"ckv{l}", 1, lambda k: C_hi[:, 2, :], xs(0))
                act.wait_ge(br_mm, 3 * l + 1)
                for t in range(2):
                    for q in range(2):
                        r = slice(64 * q, 64 * q + 64)
                        i = nc.scalar.activation(Y_hi[r, 4 + t, :], ps[r, 2 * t + q, :], ACT.Copy,
                                                 scale=V[r, VCOL[f"pool_scale{l}"] + t:VCOL[f"pool_scale{l}"] + t + 1])
                    i.then_inc(hi_ready, 1)
                act.wait_ge(br_mm, 3 * l + 2)
                for n in range(4):
                    i = nc.scalar.activation(SQ[:, 0, 0:256], ps[:, 4 + n // 2, (n % 2) * 256:(n % 2) * 256 + 256], ACT.Square,
                                             accum_out=st[:, 0, 8 + n:9 + n]).then_inc(a_chain, 1)
                    act.wait_ge(a_chain, 5 * l + n + 1)
                nc.scalar.activation(st[:, 1, 8:12], st[:, 0, 8:12], ACT.Sqrt, bias=v("eps"), scale=1.0 / 256).then_inc(a_chain, 1)
                act.wait_ge(a_chain, 5 * l + 5)
                for name in ("sgu", "conv"):
                    for k in range(2):
                        act.wait_ge(src_ready, SRC[f"{name}{l}"] + k + 1)
                        nc.scalar.activation(Y_hi[:, (6 if name == "sgu" else 8) + k, :], XS[:, k % 2, :], ACT.Copy).then_inc(hi_ready, 1)
                for u in range(U["qkv"], U["qkv"] + U_QKV):
                    tick(u)
                act.wait_ge(kr_ready, l + 1)
                for h in range(H1):
                    i = nc.scalar.activation(K1[64:96, h, :], tmp[64:96, 0, :], ACT.Copy)
                i.then_inc(kr_spread, 1)
                attention(l * H1, H1, f"att{l}", False)
                with act.Fori(0, DT // 2) as i:
                    for j in range(12):
                        c = U["merge"] + j
                        u = i * 12 + c
                        tick(u, c)
                        if j % 6 >= 2:
                            b = j % 6 - 2
                            act.wait_ge(w_used, u + 1)
                            act.wait_ge(unit_out, u + (1 - 6))
                            nc.scalar.activation(gates[:, b, :], ps[:, c % 4, :], ACT.Sigmoid).then_inc(sig_done, 1)
                for u in range(U["out"], U["out"] + U_OUT):
                    tick(u)
                norm(f"post_mix{l}", lambda k: Dn[:, k, :], (unit_out, U["out"]), D)
                norm(f"pre_ffn{l}", lambda k: X[:, k, :], (x_done, XDONE[f"post_mix{l}"]), D)
                split_src(f"pre_ffn{l}", 8, lambda k: H_hi[:, k, :], xs(0))

                def ffn(c, size, off, u0, i):
                    for j in range(size):
                        e = off + j + l * FT
                        for q in range(2):
                            tick(u0 + 2 * j + q if i is None else i * 24 + (u0 + 2 * j + q), u0 + 2 * j + q)
                        e = e if i is None else i * 8 + e
                        act.wait_ge(f_lin, e + 1)
                        nc.scalar.activation(fb[:, j % 2, :], fa[:, j % 2, :], ACT.Silu).then_inc(f_act, 1)
                        act.wait_ge(src_ready, e + (1 + SRC[f"ffn{l}"] - l * FT))
                        nc.scalar.activation(Y_hi[:, j, :], XS[:, j % 2, :], ACT.Copy).then_inc(hi_ready, 1)
                    for m in range(DT):
                        tick(u0 + 2 * size + m if i is None else i * 24 + (u0 + 2 * size + m), u0 + 2 * size + m)
                with act.Fori(0, 2) as i:
                    ffn(0, 8, 0, U["ffn"], i)
                ffn(2, 6, 16, U["ffn"] + 48, None)
                norm(f"post_ffn{l}", lambda k: Dn[:, k, :], (unit_out, U["ffn"] + U_FFN - 8), D)
            norm("a_norm", lambda k: X[:, k, :], (x_done, XDONE["post_ffn1"]), D)
            split_src("a_norm", 8, lambda k: H_hi[:, k, :], xs(0))
            for u in range(B2, B2 + 16):
                tick(u)
                if u >= B2 + 8:
                    act.wait_ge(w_used, u + 1)
                    nc.scalar.activation(gelu_g[:, u - B2 - 8, :], ps[:, u % 4, :], ACT.Gelu_apprx_tanh).then_inc(lru_act, 1)
            act.wait_ge(lru_vec, 1)
            nc.scalar.activation(sp[:, 8:16], sp[:, 0:8], ACT.Exp).then_inc(lru_act, 1)
            act.wait_ge(lru_act, 9)
            nc.scalar.activation(sp[:, 16:24], sp[:, 8:16], ACT.Ln, bias=1.0).then_inc(lru_act, 1)
            split_src("rec", 8, lambda k: Y_hi[:, k, :], lambda k: rec[:, k, :])
            for u in (UG, UG + 1):
                tick(u)
                act.wait_ge(w_used, u + 1)
                for q in range(4):
                    n = 4 * (u - UG) + q
                    nc.scalar.activation(lru_r[:, n, :], ps[:, 2 * q, :], ACT.Sigmoid, bias=v("a_bg", 2 * n))
                    nc.scalar.activation(lru_i[:, n, :], ps[:, 2 * q + 1, :], ACT.Sigmoid, bias=v("a_bg", 2 * n + 1)).then_inc(lru_act, 1)
            act.wait_ge(lru_act, 18)
            act.wait_ge(lru_vec, 2)
            for n in range(8):
                nc.scalar.activation(lru_t[:, n, :], lru_r[:, n, :], ACT.Tanh, scale=sp[:, 32 + n:33 + n]).then_inc(lru_act, 1)
            act.wait_ge(lru_act, 26)
            for n in range(8):
                nc.scalar.activation(lru_r[:, n, :], lru_r[:, n, :], ACT.Exp, scale=sp[:, 24 + n:25 + n]).then_inc(lru_act, 1)
            for n in range(8):
                act.wait_ge(lru_vec, 3 + n)
                nc.scalar.activation(lru_t[:, n, :], lru_t[:, n, :], ACT.Sqrt).then_inc(lru_act, 1)
            split_src("lru", 8, lambda k: Y_hi[:, k, :], lambda k: lru_t[:, k, :])
            for u in range(UAO, UAO + 8):
                tick(u)

            def mlp(n, U0):
                norm(f"mlp{n}", lambda k: X[:, k, :], (x_done, XDONE["a_out" if n == 0 else "b_out"]), D)
                split_src(f"mlp_in{n}", 8, lambda k: H_hi[:, k, :], xs(0))
                def quarter(i):
                    for j in range(8):
                        u = i * 16 + (U0 + j)
                        tick(u, U0 + j)
                        act.wait_ge(w_used, u + 1)
                        nc.scalar.activation(fa[:, j % 2, :], ps[:, (U0 + j) % 4, :], ACT.Relu).then_inc(f_act, 1)
                        act.wait_ge(src_ready, i * 8 + (SRC[f"mlp{n}"] + j + 1))
                        nc.scalar.activation(Y_hi[:, j, :], XS[:, j % 2, :], ACT.Copy).then_inc(hi_ready, 1)
                    for m in range(8):
                        tick(i * 16 + (U0 + 8 + m), U0 + 8 + m)
                with act.Fori(0, QUARTERS - 1) as i:
                    quarter(i)
                quarter(QUARTERS - 1)

            mlp(0, UM0)
            norm("kv_norm", lambda k: X[:, k, :], (x_done, XDONE["mlp0"]), D)
            split_src("kv_norm", 8, lambda k: H_hi[:, k, :], xs(0))

            def head_norms(u0, buf, base):
                for t in range(8):
                    tick(u0 + t)
                    act.wait_ge(unit_out, u0 + t + 1)
                    nc.scalar.activation(SQ[:, 0, :], buf[:, t, :], ACT.Square).then_inc(hn_sq, 1)
                    act.wait_ge(hn_mm, base + t + 1)
                    nc.scalar.activation(SQ[:, 1, :], ps[:, 7, :], ACT.Sqrt, bias=v("eps"), scale=1.0 / HD2).then_inc(hn_std, 1)
                    act.wait_ge(hn_done, base + t + 1)
            head_norms(UK, K1, 0)
            for u in range(UVV, UVV + 8):
                tick(u)
            split_src("b_norm", 8, lambda k: H_hi[:, k, :], xs(0))
            head_norms(UQ, Q1, 8)
            act.wait_ge(w_used, UQ + 8)
            act.dma_start(rel_bias[:], bias2).then_inc(bias_loaded, 16)
            attention(2 * H1, H2, "att2", True)
            for u in range(UO, UO + 8):
                tick(u)
            mlp(1, UM1)

        @block.tensor
        def _(pe):
            MM = nc.tensor.matmul

            def three(out, wh, wl, xh, xl, start, stop):
                MM(out, wh, xh, start=start, stop=False)
                MM(out, wh, xl, start=False, stop=False)
                return MM(out, wl, xh, start=False, stop=stop)

            def unit(u, c, out, xh, xl, tiles, free, tail=None):
                pe.wait_ge(w_lo_ready, u + 1)
                if free is not None:
                    pe.wait_ge(unit_out, free)
                s = c % WSLOTS
                for k in range(tiles):
                    m = three(out, w_hi[:, s, k * P:(k + 1) * P], w_lo[:, s, k * P:(k + 1) * P], xh(k), xl(k), k == 0, k == tiles - 1)
                m.then_inc(w_used, 1)

            Hh, Hl = (lambda k: H_hi[:, k, :]), (lambda k: H_lo[:, k, :])
            Yh, Yl = (lambda k: Y_hi[:, k, :]), (lambda k: Y_lo[:, k, :])

            def gemm(u0, n, xh, xl, tiles=8):
                for u in range(u0, u0 + n):
                    unit(u, u, ps[:, u % 4, :], xh, xl, tiles, u - 3 if u >= 4 else None)

            def norm(name):
                n, b, t = NORMS[name]
                pe.wait_ge(sq_added, b + t)
                if n:
                    pe.wait_ge(std_ready, n)
                MM(ps[:, 7, :], ones[:], ACC[:], start=True, stop=True).then_inc(ssum_ready, 1)

            def attention(g0, heads, second):
                pb = [4, 5, 6, 6]
                col = [0, 0, 0, 256]
                Vt, pr, prT = (V2, probs2, probsT2) if second else (V1, probs, probsT)

                def scores(g):
                    h = g - g0
                    if g > g0:
                        pe.wait_ge(s_free if second else exp_done, g - g0 if second else g)
                    for j in range(4):
                        w = P * (j + 1)
                        r = slice(64 * (h % 2), 64 * (h % 2) + 64) if second else slice(0, QK)
                        t = h // 2 if second else h
                        MM(ps[:, j, 0:w], Q1[r, t, j * P:(j + 1) * P], K1[r, t, 0:w], start=True, stop=False)
                        m = MM(ps[:, j, j * P:w], sel_row[0:1, :], neg_row[0:1, :], start=False, stop=True)
                    m.then_inc(s_ready, 1)
                scores(g0)
                for g in range(g0, g0 + heads):
                    h = g - g0
                    if h + 1 < heads:
                        scores(g + 1)
                    pe.wait_ge(p_ready, g + 1)
                    if g:
                        pe.wait_ge(pt_a, g)
                        pe.wait_ge(pt_v, g)
                    off = 0
                    for j in range(4):
                        for i in range(j + 1):
                            c0 = col[i] + (j - i) * P
                            m = nc.tensor.transpose(ps[:, pb[i], c0:c0 + P], pr[:, g % 2, off + i * P:off + (i + 1) * P], ident[:])
                        off += (j + 1) * P
                    m.then_inc(t_done, 1)
                    pe.wait_ge(pt_a, g + 1)
                    pe.wait_ge(pt_v, g + 1)
                    if g > g0:
                        pe.wait_ge(lo_ready, SPLIT["att2" if second else f"att{g0 // H1}"] + h)
                    r = slice(64 * (h % 2), 64 * (h % 2) + 64)
                    o = 0
                    for i in range(4):
                        n = S - i * P
                        m = MM(ps[r, 7, i * P:S], Vt[:, i, h * 64:(h + 1) * 64], prT[:, o:o + n], start=i == 0, stop=i == 3)
                        o += n
                    m.then_inc(pv_done, 1)

            pe.wait_ge(consts_made, 10)
            for l in range(L1):
                U = first_units(l)
                norm(f"pre_mix{l}")
                pe.wait_ge(lo_ready, SPLIT[f"pre_mix{l}"] + 8)
                gemm(U["win"], U_IN, Hh, Hl)
                norm(f"cq{l}")
                norm(f"ckv{l}")
                pe.wait_ge(layer_loaded, 64 * (l + 1))
                pe.wait_ge(br_vec, 3 * l + 1)
                for g in range(4):
                    r = slice(64 * (g % 2), 64 * (g % 2) + 64)
                    m = MM(ps[r, g, :], poolw[r, g // 2, :], (SA, SB)[g % 2][r, g // 2, 16:528], start=True, stop=True)
                m.then_inc(br_mm, 1)
                for n in range(4):
                    for t in range(2):
                        c0 = (n % 2) * 256 + t * P
                        m = nc.tensor.transpose(ps[:, 4 + n // 2, c0:c0 + P], A[:, 8 + t, n * P:(n + 1) * P], ident[:])
                m.then_inc(br_mm, 1)
                pe.wait_ge(br_vec, 3 * l + 3)
                for g in range(4):
                    r = slice(64 * (g % 2), 64 * (g % 2) + 64)
                    for n in range(4):
                        m = MM(ps[r, 6 + g // 2, n * P:(n + 1) * P], vnT[:, n, g * 64:(g + 1) * 64], sguw[:, g, :], start=True, stop=True)
                m.then_inc(br_mm, 1)
                uq = U["qkv"]
                pe.wait_ge(lo_ready, SPLIT[f"conv{l}"] + 2)
                for q in range(2):
                    u = uq + q
                    pe.wait_ge(w_lo_ready, u + 1)
                    if q:
                        pe.wait_ge(qk_out, 20 * l + 4)
                    for b in range(4):
                        for k in range(2):
                            c0 = (2 * b + k) * P
                            m = three(ps[:, b, :], w_hi[:, u % 4, c0:c0 + P], w_lo[:, u % 4, c0:c0 + P], C_hi[:, k, :], C_lo[:, k, :], k == 0, k == 1)
                    m.then_inc(w_used, 1)
                u = uq + 2
                pe.wait_ge(w_lo_ready, u + 1)
                for h in range(8):
                    if h < 4:
                        pe.wait_ge(qk_out, 20 * l + 8)
                    c0 = h * P
                    m = three(ps[:, h, :], w_hi[:, u % 4, c0:c0 + P], w_lo[:, u % 4, c0:c0 + P], C_hi[:, 2, :], C_lo[:, 2, :], True, True)
                m.then_inc(qk_mm, 1)
                pe.wait_ge(qk_out, 20 * l + 12)
                wh = w_hi[:, u % 4, :].rearrange("p (h c) -> p h c", c=P)[:, :, 64:128]
                wl = w_lo[:, u % 4, :].rearrange("p (h c) -> p h c", c=P)[:, :, 64:128]
                for i in range(4):
                    o = ps[:, i, :].rearrange("p (h c) -> p h c", c=64)
                    t = slice(i * P, (i + 1) * P)
                    MM(o, C_hi[:, 2, t], wh, start=True, stop=False)
                    MM(o, C_hi[:, 2, t], wl, start=False, stop=False)
                    m = MM(o, C_lo[:, 2, t], wh, start=False, stop=True)
                m.then_inc(w_used, 1)
                pe.wait_ge(qk_out, 20 * (l + 1))
                pe.wait_ge(kr_spread, l + 1)
                attention(l * H1, H1, False)
                pe.wait_ge(lo_ready, SPLIT[f"att{l}"] + H1)
                with pe.Fori(0, DT // 2) as i:
                    for j in range(12):
                        c = U["merge"] + j
                        u = i * 12 + c
                        s = c % 4
                        if j % 6 < 2:
                            pe.wait_ge(w_lo_ready, u + 1)
                            pe.wait_ge(unit_out, u - 3)
                            parts = ((4, 0, (0, 1, 2, 3)), (5, 4, (4, 5))) if j % 6 == 0 else ((6, 0, (6, 7)), (7, 2, (8, 9)))
                            for bank, w0, ks in parts:
                                for n, k in enumerate(ks):
                                    c0 = (w0 + n) * P
                                    m = three(ps[:, bank, :], w_hi[:, s, c0:c0 + P], w_lo[:, s, c0:c0 + P], Y_hi[:, k, :], Y_lo[:, k, :], n == 0, n == len(ks) - 1)
                            m.then_inc(w_used, 1)
                        else:
                            unit(u, c, ps[:, c % 4, :], Hh, Hl, 8, u - 3)
                pe.wait_ge(merged_lo, DT * (l + 1))
                gemm(U["out"], U_OUT, lambda k: M_hi[:, k, :], lambda k: M_lo[:, k, :])
                norm(f"post_mix{l}")
                norm(f"pre_ffn{l}")
                pe.wait_ge(lo_ready, SPLIT[f"pre_ffn{l}"] + 8)

                def ffn(size, u0, i, e):
                    for j in range(2 * size):
                        u = u0 + j if i is None else i * 24 + (u0 + j)
                        unit(u, u0 + j, ps[:, (u0 + j) % 4, :], Hh, Hl, 8, u - 3)
                    pe.wait_ge(lo_ready, (e + size) if i is None else i * 8 + (e + size))
                    for m in range(8):
                        c = u0 + 2 * size + m
                        u = c if i is None else i * 24 + c
                        unit(u, c, ps[:, c % 4, :], Yh, Yl, size, u - 3)
                with pe.Fori(0, 2) as i:
                    ffn(8, U["ffn"], i, SPLIT[f"ffn{l}"])
                ffn(6, U["ffn"] + 48, None, SPLIT[f"ffn{l}"] + 16)
                norm(f"post_ffn{l}")
            norm("a_norm")
            pe.wait_ge(lo_ready, SPLIT["a_norm"] + 8)
            gemm(B2, 16, Hh, Hl)
            pe.wait_ge(lo_ready, SPLIT["rec"] + 8)
            for u in (UG, UG + 1):
                pe.wait_ge(w_lo_ready, u + 1)
                pe.wait_ge(unit_out, UG)
                if u > UG:
                    pe.wait_ge(lru_act, 14)
                for q in range(4):
                    n = 4 * (u - UG) + q
                    for e in range(2):
                        c0 = (2 * q + e) * P
                        m = three(ps[:, 2 * q + e, :], w_hi[:, u % 4, c0:c0 + P], w_lo[:, u % 4, c0:c0 + P], Y_hi[:, n, :], Y_lo[:, n, :], True, True)
                m.then_inc(w_used, 1)
            pe.wait_ge(lo_ready, SPLIT["lru"] + 8)
            gemm(UAO, 8, Yh, Yl)

            def mlp(n, U0):
                norm(f"mlp{n}")
                pe.wait_ge(lo_ready, SPLIT[f"mlp_in{n}"] + 8)
                with pe.Fori(0, QUARTERS) as i:
                    for j in range(8):
                        unit(i * 16 + (U0 + j), U0 + j, ps[:, (U0 + j) % 4, :], Hh, Hl, 8, i * 16 + (U0 + j - 3))
                    pe.wait_ge(lo_ready, i * 8 + (SPLIT[f"mlp{n}"] + 8))
                    for m in range(8):
                        c = U0 + 8 + m
                        unit(i * 16 + c, c, ps[:, c % 4, :], Yh, Yl, 8, i * 16 + (c - 3))
            mlp(0, UM0)
            norm("kv_norm")
            pe.wait_ge(lo_ready, SPLIT["kv_norm"] + 8)

            def head_norm(t):
                pe.wait_ge(hn_sq, t + 1)
                MM(ps[:, 7, :], ones64[:], SQ[:, 0, :], start=True, stop=True).then_inc(hn_mm, 1)
            for u in range(UK, UK + 8):
                unit(u, u, ps[:, u % 4, :], Hh, Hl, 8, u - 3)
                if u > UK:
                    head_norm(u - UK - 1)
            head_norm(7)
            for half in range(2):
                for q in range(4):
                    u = UVV + 4 * half + q
                    pe.wait_ge(w_lo_ready, u + 1)
                    if q == 0:
                        pe.wait_ge(unit_out, u)
                    for k in range(2):
                        wh, wl = w_hi[:, u % 4, k * S:(k + 1) * S], w_lo[:, u % 4, k * S:(k + 1) * S]
                        for i in range(4):
                            t = slice(i * P, (i + 1) * P)
                            first, last = q == 0 and k == 0, q == 3 and k == 1
                            MM(ps[:, i, :], H_hi[:, 2 * q + k, t], wh, start=first, stop=False)
                            MM(ps[:, i, :], H_hi[:, 2 * q + k, t], wl, start=False, stop=False)
                            m = MM(ps[:, i, :], H_lo[:, 2 * q + k, t], wh, start=False, stop=last)
                    m.then_inc(w_used, 1)
            pe.wait_ge(lo_ready, SPLIT["b_norm"] + 8)
            pe.wait_ge(unit_out, UQ)
            for u in range(UQ, UQ + 8):
                unit(u, u, ps[:, u % 4, :], Hh, Hl, 8, u - 3)
                if u > UQ:
                    head_norm(8 + u - UQ - 1)
            head_norm(15)
            pe.wait_ge(hn_done, 16)
            attention(2 * H1, H2, True)
            pe.wait_ge(lo_ready, SPLIT["att2"] + H2)
            gemm(UO, 8, Yh, Yl)
            mlp(1, UM1)

        @block.vector
        def _(dve):
            VE = nc.vector
            links = [0]

            def link(ins):
                links[0] += 1
                ins.then_inc(chain, 1)
                dve.wait_ge(chain, links[0])

            def looped(n, per, body):
                base = links[0]
                with dve.Fori(0, n) as i:
                    k = [0]

                    def lk(ins):
                        k[0] += 1
                        ins.then_inc(chain, 1)
                        dve.wait_ge(chain, i * per + (base + k[0]))
                    body(i, lk)
                assert k[0] == per, (k[0], per)
                links[0] = base + n * per

            def out_of(u):
                dve.sem_inc(unit_out, 1)

            def norm(name, d, src, gain, dst_lo=None, dst_hi=None, split=None, after=None):
                n, b, t = NORMS[name]
                for k in range(t):
                    dve.wait_ge(sq_ready, b + k + 1)
                    if k == 0:
                        i = VE.tensor_copy(ACC[:], SQ[:, (b + k) % 2, :])
                    else:
                        i = VE.tensor_tensor(ACC[:], ACC[:], SQ[:, (b + k) % 2, :], ALU.add)
                    i.then_inc(sq_added, 1)
                    dve.wait_ge(sq_added, b + k + 1)
                dve.wait_ge(std_ready, n + 1)
                link(VE.reciprocal(RS[:], SQ[:, (b + t) % 2, :]))
                if split is not None:
                    scale_split(split, t, src, gain, dst_hi, dst_lo)

            def scale_split(split, t, src, gain, dst_hi, dst_lo):
                s0 = SPLIT[split]

                def lo(k):
                    dve.wait_ge(hi_ready, s0 + k + 1)
                    VE.tensor_tensor(dst_lo(k), XS[:, k % 2, :], f(dst_hi(k)), ALU.subtract).then_inc(lo_ready, 1)
                    dve.wait_ge(lo_ready, s0 + k + 1)
                for k in range(t):
                    VE.scalar_tensor_tensor(XS[:, k % 2, :], src(k), gain(k), RS[:], ALU.mult, ALU.mult).then_inc(src_ready, 1)
                    dve.wait_ge(src_ready, SRC[split] + k + 1)
                    if k:
                        lo(k - 1)
                lo(t - 1)

            def post_norm(name, l):
                norm(name, D, None, None)
                for k in range(DT):
                    link(VE.scalar_tensor_tensor(XS[:, k % 2, :], Dn[:, k, :], v(name, k), RS[:], ALU.mult, ALU.mult))
                    VE.tensor_tensor(X[:, k, :], X[:, k, :], XS[:, k % 2, :], ALU.add).then_inc(x_done, 1)
                    dve.wait_ge(x_done, XDONE[name] + k + 1)

            def copy_out(u, dst, bank=None):
                dve.wait_ge(w_used, u + 1)
                VE.tensor_copy(dst, ps[:, u % 4 if bank is None else bank, :]).then_inc(unit_out, 1)
                dve.wait_ge(unit_out, u + 1)

            def attention(g0, heads, split, second):
                pr, prT = (probs2, probsT2) if second else (probs, probsT)

                def maxima(g):
                    h = g - g0
                    dve.wait_ge(s_ready, g + 1)
                    if second:
                        dve.wait_ge(t_done, g - 1)
                        off = 0
                        for j in range(4):
                            w = P * (j + 1)
                            far = max(0, w - 2 * P)
                            near = w - far
                            link(VE.scalar_tensor_tensor(pr[:, g % 2, off + far:off + w], ps[:, j, far:w], HD2 ** -0.5,
                                                         rel_bias[:, h, 2 * P - near:2 * P], ALU.mult, ALU.add))
                            if far:
                                i = VE.tensor_scalar(pr[:, g % 2, off:off + far], ps[:, j, 0:far], HD2 ** -0.5,
                                                     rel_bias[:, h, 0:1], ALU.mult, ALU.add)
                                link(i) if j < 3 else i.then_inc(s_free, 1)
                            off += w
                        dve.wait_ge(s_free, g - g0 + 1)
                        off = 0
                        for j in range(4):
                            w = P * (j + 1)
                            link(VE.tensor_reduce(st[:, g % 2, 8 + j:9 + j], pr[:, g % 2, off:off + w], AX.X, ALU.max))
                            off += w
                        VE.tensor_scalar(st[:, g % 2, 0:4], st[:, g % 2, 8:12], -1.0, None, ALU.mult).then_inc(max_ready, 1)
                    else:
                        for j in range(4):
                            link(VE.tensor_reduce(st[:, g % 2, 8 + j:9 + j], ps[:, j, 0:P * (j + 1)], AX.X, ALU.max))
                        VE.tensor_scalar(st[:, g % 2, 0:4], st[:, g % 2, 8:12], -(QK ** -0.5), None, ALU.mult).then_inc(max_ready, 1)
                    dve.wait_ge(max_ready, g + 1)
                maxima(g0)
                for g in range(g0, g0 + heads):
                    h = g - g0
                    dve.wait_ge(exp_done, g + 1)
                    link(VE.reciprocal(st[:, g % 2, 12:16], st[:, g % 2, 4:8]))
                    off = 0
                    for j in range(4):
                        w = P * (j + 1)
                        o = pr[:, g % 2, off:off + w]
                        i = VE.tensor_scalar(o, o, st[:, g % 2, 12 + j:13 + j], None, ALU.mult)
                        if j < 3:
                            link(i)
                        off += w
                    i.then_inc(p_ready, 1)
                    dve.wait_ge(p_ready, g + 1)
                    if h + 1 < heads:
                        maxima(g + 1)
                    dve.wait_ge(t_done, g + 1)
                    if g:
                        dve.wait_ge(pv_done, g)
                    link(VE.tensor_copy(prT[:, S:S + 384], ps[:, 5, 0:384]))
                    VE.tensor_copy(prT[:, S + 384:1280], ps[:, 6, 0:384]).then_inc(pt_v, 1)
                    dve.wait_ge(pt_v, g + 1)
                    r = slice(64 * (h % 2), 64 * (h % 2) + 64)
                    dve.wait_ge(hi_ready, SPLIT[split] + h + 1)
                    VE.tensor_tensor(Y_lo[r, h // 2, :], ps[r, 7, :], f(Y_hi[r, h // 2, :]), ALU.subtract).then_inc(lo_ready, 1)
                    dve.wait_ge(lo_ready, SPLIT[split] + h + 1)

            def lo_of(split, k, dst, src, hi):
                dve.wait_ge(hi_ready, SPLIT[split] + k + 1)
                VE.tensor_tensor(dst, src, f(hi), ALU.subtract).then_inc(lo_ready, 1)
                dve.wait_ge(lo_ready, SPLIT[split] + k + 1)

            dve.wait_ge(consts_loaded, 48)
            for l in range(L1):
                U = first_units(l)
                norm(f"pre_mix{l}", D, lambda k: X[:, k, :], lambda k: v(f"pre_mix{l}", k), lambda k: H_lo[:, k, :], lambda k: H_hi[:, k, :], f"pre_mix{l}")
                for u in range(U["win"], U["win"] + U_IN):
                    copy_out(u, A[:, u - U["win"], :])
                norm(f"cq{l}", 256, lambda k: A[:, k, :], lambda k: v(f"cq{l}", k), lambda k: C_lo[:, k, :], lambda k: C_hi[:, k, :], f"cq{l}")
                norm(f"ckv{l}", 128, lambda k: A[:, 2, :], lambda k: v(f"ckv{l}", k), lambda k: C_lo[:, 2, :], lambda k: C_hi[:, 2, :], f"ckv{l}")
                link(VE.memset(Z[:, :, 0:16], 0.0))
                link(VE.tensor_copy(Z[:, :, 16:528], A[:, 4:6, :]))
                link(VE.tensor_tensor(SA[:, :, 1:528], Z[:, :, 1:528], Z[:, :, 0:527], ALU.add))
                link(VE.tensor_tensor(SB[:, :, 3:528], SA[:, :, 3:528], SA[:, :, 1:526], ALU.add))
                link(VE.tensor_tensor(SA[:, 1, 7:528], SB[:, 1, 7:528], SB[:, 1, 3:524], ALU.add))
                link(VE.tensor_tensor(SB[64:128, 1, 15:528], SA[64:128, 1, 15:528], SA[64:128, 1, 7:520], ALU.add))
                for q, W in ((0, SA), (1, SB)):
                    r = slice(64 * q, 64 * q + 64)
                    link(VE.tensor_tensor(W[r, :, 16:32], W[r, :, 16:32], winfix[r, :, :], ALU.mult))
                    for t in range(2):
                        link(VE.scalar_tensor_tensor(W[r, t, 16:528], W[r, t, 16:528], V[r, VCOL["inv_win"] + t:VCOL["inv_win"] + t + 1],
                                                     A[r, 4 + t, :], ALU.mult, ALU.subtract))
                dve.sem_inc(br_vec, 1)
                link(VE.memset(Z[:, :, 0:2], 0.0))
                link(VE.tensor_tensor(Z[:, :, 2:514], A[:, 12:14, :], A[:, 14:16, :], ALU.mult))
                cw = VCOL[f"conv{l}"]
                for t in range(2):
                    link(VE.tensor_scalar(XS[:, t, :], Z[:, t, 2:514], V[:, cw + 4 + t:cw + 5 + t], None, ALU.mult))
                    link(VE.scalar_tensor_tensor(XS[:, t, :], Z[:, t, 1:513], V[:, cw + 2 + t:cw + 3 + t], XS[:, t, :], ALU.mult, ALU.add))
                    link(VE.scalar_tensor_tensor(XS[:, t, :], Z[:, t, 0:512], V[:, cw + t:cw + 1 + t], XS[:, t, :], ALU.mult, ALU.add))
                link(VE.tensor_tensor(A[:, 10:12, :], A[:, 10:12, :], XS[:, :, :], ALU.mult))
                for t in range(2):
                    dve.wait_ge(hi_ready, SPLIT[f"pool{l}"] + t + 1)
                    for q in range(2):
                        r = slice(64 * q, 64 * q + 64)
                        i = VE.scalar_tensor_tensor(Y_lo[r, 4 + t, :], ps[r, 2 * t + q, :], V[r, VCOL[f"pool_scale{l}"] + t:VCOL[f"pool_scale{l}"] + t + 1],
                                                    f(Y_hi[r, 4 + t, :]), ALU.mult, ALU.subtract)
                        if q == 0:
                            link(i)
                    i.then_inc(lo_ready, 1)
                    dve.wait_ge(lo_ready, SPLIT[f"pool{l}"] + t + 1)
                dve.wait_ge(layer_loaded, 64 * (l + 1))
                VE.memset(sguw[64:128, :, 0:64], 0.0).then_inc(br_vec, 1)
                dve.wait_ge(br_vec, 3 * l + 2)
                dve.wait_ge(a_chain, 5 * l + 5)
                link(VE.reciprocal(st[:, 0, 12:16], st[:, 1, 8:12]))
                for n in range(4):
                    i = VE.scalar_tensor_tensor(vnT[:, n, :], ps[:, 4 + n // 2, (n % 2) * 256:(n % 2) * 256 + 256], st[:, 0, 12 + n:13 + n],
                                                sgug[:], ALU.mult, ALU.mult)
                    if n < 3:
                        link(i)
                i.then_inc(br_vec, 1)
                dve.wait_ge(br_vec, 3 * l + 3)
                dve.wait_ge(br_mm, 3 * l + 3)
                for t in range(2):
                    pm = ps[:, 6 + t, :].rearrange("p (n i) -> p n i", i=P)
                    bb = sgub[:, t:t + 1, :].to_broadcast([P, 4, P])
                    link(VE.tensor_tensor(XS[:, t, :].rearrange("p (n i) -> p n i", i=P), pm, bb, ALU.add))
                    VE.tensor_tensor(XS[:, t, :], XS[:, t, :], A[:, 6 + t, :], ALU.mult).then_inc(src_ready, 1)
                    dve.wait_ge(src_ready, SRC[f"sgu{l}"] + t + 1)
                for t in range(2):
                    lo_of(f"sgu{l}", t, Y_lo[:, 6 + t, :], XS[:, t, :], Y_hi[:, 6 + t, :])
                for t in range(2):
                    VE.tensor_copy(XS[:, t, :], A[:, 10 + t, :]).then_inc(src_ready, 1)
                    dve.wait_ge(src_ready, SRC[f"conv{l}"] + t + 1)
                link(VE.tensor_tensor(tmp[64:96, 0, :], A[64:96, 3, :], CS[64:96, :], ALU.mult))
                link(VE.tensor_tensor(tmp[64:96, 1, :], A[96:128, 3, :], CS[96:128, :], ALU.mult))
                VE.tensor_tensor(tmp[64:96, 0, :], tmp[64:96, 0, :], tmp[64:96, 1, :], ALU.add).then_inc(kr_ready, 1)
                dve.wait_ge(kr_ready, l + 1)
                for t in range(2):
                    lo_of(f"conv{l}", t, Y_lo[:, 8 + t, :], XS[:, t, :], Y_hi[:, 8 + t, :])
                for q in range(2):
                    u = U["qkv"] + q
                    dve.wait_ge(w_used, u + 1)
                    for b in range(4):
                        h = 4 * q + b
                        link(VE.tensor_tensor(Q1[0:96, h, :], ps[0:96, b, :], CS[0:96, :], ALU.mult))
                        link(VE.tensor_tensor(tmp[64:96, 1, :], ps[96:128, b, :], CS[96:128, :], ALU.mult))
                        VE.tensor_tensor(Q1[64:96, h, :], Q1[64:96, h, :], tmp[64:96, 1, :], ALU.add).then_inc(qk_out, 1)
                        dve.wait_ge(qk_out, 20 * l + h + 1)
                    out_of(u)
                dve.wait_ge(qk_mm, l + 1)
                for h in range(8):
                    VE.tensor_copy(K1[0:64, h, :], ps[0:64, h, :]).then_inc(qk_out, 1)
                    dve.wait_ge(qk_out, 20 * l + 9 + h)
                dve.wait_ge(w_used, U["qkv"] + 3)
                for i_ in range(4):
                    VE.tensor_copy(V1[:, i_, :], ps[:, i_, :]).then_inc(qk_out, 1)
                    dve.wait_ge(qk_out, 20 * l + 17 + i_)
                out_of(U["qkv"] + 2)
                attention(l * H1, H1, f"att{l}", False)

                def merge(i, lk):
                    for m in range(2):
                        for y in range(2):
                            c = U["merge"] + 6 * m + y
                            dve.wait_ge(w_used, i * 12 + (c + 1))
                            lk(VE.tensor_scalar(ysb[:, 2 * y, :], ps[:, 4 + 2 * y, :], 1.0, None, ALU.mult))
                            VE.tensor_scalar(ysb[:, 2 * y + 1, :], ps[:, 5 + 2 * y, :], 1.0, None, ALU.mult).then_inc(unit_out, 1)
                            dve.wait_ge(unit_out, i * 12 + (c + 1))
                        for b in range(4):
                            c = U["merge"] + 6 * m + 2 + b
                            dve.wait_ge(sig_done, i * 8 + (l * 32 + 4 * m + b + 1))
                            o = tmp[:, m, :] if b == 0 else XS[:, 0, :]
                            VE.tensor_tensor(o, gates[:, b, :], ysb[:, b, :], ALU.mult).then_inc(unit_out, 1)
                            dve.wait_ge(unit_out, i * 12 + (c + 1))
                            if b:
                                lk(VE.tensor_tensor(tmp[:, m, :], tmp[:, m, :], XS[:, 0, :], ALU.add))
                        lk(VE.tensor_scalar(M_hi[:, i * 2 + m, :], tmp[:, m, :], 1.0, None, ALU.mult))
                        VE.tensor_tensor(M_lo[:, i * 2 + m, :], tmp[:, m, :], f(M_hi[:, i * 2 + m, :]), ALU.subtract).then_inc(merged_lo, 1)
                        dve.wait_ge(merged_lo, i * 2 + (l * DT + m + 1))
                looped(DT // 2, 2 * 6, merge)
                for u in range(U["out"], U["out"] + U_OUT):
                    copy_out(u, Dn[:, u - U["out"], :])
                post_norm(f"post_mix{l}", l)
                norm(f"pre_ffn{l}", D, lambda k: X[:, k, :], lambda k: v(f"pre_ffn{l}", k), lambda k: H_lo[:, k, :], lambda k: H_hi[:, k, :], f"pre_ffn{l}")

                def ffn(size, u0, i, off, lk, first):
                    st_ = 24
                    at_ = (lambda c: c) if i is None else (lambda c: i * st_ + c)
                    e_ = (lambda c: c) if i is None else (lambda c: i * 8 + c)
                    for j in range(size):
                        dve.wait_ge(w_used, at_(u0 + 2 * j + 1))
                        VE.tensor_copy(fa[:, j % 2, :], ps[:, (u0 + 2 * j) % 4, :]).then_inc(f_lin, 1)
                        dve.wait_ge(f_lin, e_(l * FT + off + j + 1))
                        dve.sem_inc(unit_out, 1)
                        dve.wait_ge(w_used, at_(u0 + 2 * j + 2))
                        dve.wait_ge(f_act, e_(l * FT + off + j + 1))
                        VE.tensor_tensor(XS[:, j % 2, :], fb[:, j % 2, :], ps[:, (u0 + 2 * j + 1) % 4, :], ALU.mult).then_inc(src_ready, 1)
                        k0 = SPLIT[f"ffn{l}"] + off + j + 1
                        dve.wait_ge(src_ready, e_(SRC[f"ffn{l}"] + off + j + 1))
                        dve.sem_inc(unit_out, 1)
                        dve.wait_ge(hi_ready, e_(k0))
                        VE.tensor_tensor(Y_lo[:, j, :], XS[:, j % 2, :], f(Y_hi[:, j, :]), ALU.subtract).then_inc(lo_ready, 1)
                        dve.wait_ge(lo_ready, e_(k0))
                    for m in range(8):
                        c = u0 + 2 * size + m
                        dve.wait_ge(w_used, at_(c + 1))
                        VE.tensor_tensor(Dn[:, m, :], Dn[:, m, :], ps[:, c % 4, :], ALU.add).then_inc(unit_out, 1)
                        dve.wait_ge(unit_out, at_(c + 1))
                link(VE.memset(Dn[:], 0.0))
                looped(2, 0, lambda i, lk: ffn(8, U["ffn"], i, 0, lk, False))
                ffn(6, U["ffn"] + 48, None, 16, link, False)
                post_norm(f"post_ffn{l}", l)
            norm("a_norm", D, lambda k: X[:, k, :], lambda k: v("a_norm", k), lambda k: H_lo[:, k, :], lambda k: H_hi[:, k, :], "a_norm")
            link(VE.memset(recp[:, :, 0:3], 0.0))
            for k in range(8):
                u = B2 + k
                copy_out(u, recp[:, k, 3:515])
                link(VE.tensor_scalar(rec[:, k, :], recp[:, k, 3:515], v("a_conv", 24 + k), v("a_conv_b", k), ALU.mult, ALU.add))
                for j in (2, 1):
                    link(VE.scalar_tensor_tensor(rec[:, k, :], recp[:, k, j:j + S], v("a_conv", 8 * j + k), rec[:, k, :], ALU.mult, ALU.add))
                VE.scalar_tensor_tensor(rec[:, k, :], recp[:, k, 0:S], v("a_conv", k), rec[:, k, :], ALU.mult, ALU.add).then_inc(src_ready, 1)
                dve.wait_ge(src_ready, SRC["rec"] + k + 1)
            for k in range(8):
                dve.wait_ge(lru_act, k + 1)
                dve.sem_inc(unit_out, 1)
            link(VE.tensor_scalar(sp[:, 24:32], v("a_lam", 0, 8), -1.0, None, ALU.mult))
            link(VE.tensor_tensor(sp[:, 0:8], sp[:, 24:32], v("a_lam", 0, 8), ALU.min))
            VE.tensor_scalar(sp[:, 32:40], sp[:, 24:32], 0.0, None, ALU.max).then_inc(lru_vec, 1)
            dve.wait_ge(lru_vec, 1)
            dve.wait_ge(lru_act, 10)
            link(VE.tensor_tensor(sp[:, 24:32], sp[:, 16:24], sp[:, 32:40], ALU.add))
            link(VE.tensor_scalar(sp[:, 32:40], sp[:, 24:32], 8.0, None, ALU.mult))
            VE.tensor_scalar(sp[:, 24:32], sp[:, 32:40], -1.0, None, ALU.mult).then_inc(lru_vec, 1)
            dve.wait_ge(lru_vec, 2)
            for k in range(8):
                lo_of("rec", k, Y_lo[:, k, :], rec[:, k, :], Y_hi[:, k, :])
            for q in range(2):
                dve.wait_ge(lru_act, 14 + 4 * q)
                dve.sem_inc(unit_out, 1)
            for n in range(8):
                dve.wait_ge(lru_act, 19 + n)
                link(VE.tensor_scalar(lru_u[:], lru_t[:, n, :], 1.0, None, ALU.add))
                link(VE.reciprocal(RS[:], lru_u[:]))
                VE.scalar_tensor_tensor(lru_t[:, n, :], lru_t[:, n, :], 2.0, RS[:], ALU.mult, ALU.mult).then_inc(lru_vec, 1)
                dve.wait_ge(lru_vec, 3 + n)
                link(VE.tensor_tensor(lru_i[:, n, :], lru_i[:, n, :], rec[:, n, :], ALU.mult))
            for n in range(8):
                dve.wait_ge(lru_act, 35 + n)
                link(VE.tensor_tensor(lru_i[:, n, :], lru_i[:, n, :], lru_t[:, n, :], ALU.mult))
                link(VE.tensor_tensor_scan(lru_u[:], lru_r[:, n, :], lru_i[:, n, :], 0.0, ALU.mult, ALU.add))
                VE.tensor_tensor(lru_t[:, n, :], lru_u[:], gelu_g[:, n, :], ALU.mult).then_inc(src_ready, 1)
                dve.wait_ge(src_ready, SRC["lru"] + n + 1)
            for n in range(8):
                lo_of("lru", n, Y_lo[:, n, :], lru_t[:, n, :], Y_hi[:, n, :])

            def add_to_x(u, k, name, waits=True):
                dve.wait_ge(w_used, u + 1)
                VE.tensor_tensor(X[:, k, :], X[:, k, :], ps[:, u % 4, :], ALU.add).then_inc(x_done, 1)
                dve.wait_ge(x_done, XDONE[name] + k + 1)
                dve.sem_inc(unit_out, 1)
            for k in range(8):
                add_to_x(UAO + k, k, "a_out")

            def mlp(n, U0):
                norm(f"mlp{n}", D, lambda k: X[:, k, :], lambda k: v(f"mlp{n}", k), lambda k: H_lo[:, k, :], lambda k: H_hi[:, k, :], f"mlp_in{n}")

                def ups(i):
                    for j in range(8):
                        dve.wait_ge(f_act, i * 8 + (L1 * FT + n * 32 + j + 1))
                        dve.sem_inc(unit_out, 1)
                        k0 = SPLIT[f"mlp{n}"] + j + 1
                        VE.tensor_tensor(XS[:, j % 2, :], fa[:, j % 2, :], fa[:, j % 2, :], ALU.mult).then_inc(src_ready, 1)
                        dve.wait_ge(src_ready, i * 8 + (SRC[f"mlp{n}"] + j + 1))
                        dve.wait_ge(hi_ready, i * 8 + k0)
                        VE.tensor_tensor(Y_lo[:, j, :], XS[:, j % 2, :], f(Y_hi[:, j, :]), ALU.subtract).then_inc(lo_ready, 1)
                        dve.wait_ge(lo_ready, i * 8 + k0)

                def body(i, lk):
                    ups(i)
                    for m in range(8):
                        c = U0 + 8 + m
                        dve.wait_ge(w_used, i * 16 + (c + 1))
                        VE.tensor_tensor(X[:, m, :], X[:, m, :], ps[:, c % 4, :], ALU.add).then_inc(unit_out, 1)
                        dve.wait_ge(unit_out, i * 16 + (c + 1))
                looped(QUARTERS, 0, body)
                for k in range(8):
                    dve.sem_inc(x_done, 1)

            mlp(0, UM0)
            norm("kv_norm", D, lambda k: X[:, k, :], lambda k: v("kv_norm", k), lambda k: H_lo[:, k, :], lambda k: H_hi[:, k, :], "kv_norm")

            def head_norms(u0, buf, base, gain):
                for t in range(8):
                    copy_out(u0 + t, buf[:, t, :])
                    dve.wait_ge(hn_std, base + t + 1)
                    link(VE.reciprocal(XS[:, 0, :], SQ[:, 1, :]))
                    VE.scalar_tensor_tensor(buf[:, t, :], buf[:, t, :], v(gain), XS[:, 0, :], ALU.mult, ALU.mult).then_inc(hn_done, 1)
                    dve.wait_ge(hn_done, base + t + 1)
            head_norms(UK, K1, 0, "k_norm")
            for half in range(2):
                for q in range(3):
                    dve.sem_inc(unit_out, 1)
                dve.wait_ge(w_used, UVV + 4 * half + 4)
                for i_ in range(4):
                    link(VE.tensor_copy(V2[:, i_, half * S:(half + 1) * S], ps[:, i_, :]))
                dve.sem_inc(unit_out, 1)
            scale_split("b_norm", 8, lambda k: X[:, k, :], lambda k: v("b_norm", k), lambda k: H_hi[:, k, :], lambda k: H_lo[:, k, :])
            head_norms(UQ, Q1, 8, "q_norm")
            dve.wait_ge(bias_loaded, 16)
            attention(2 * H1, H2, "att2", True)
            for k in range(8):
                add_to_x(UO + k, k, "b_out")
            mlp(1, UM1)


def lay_out(inp):
    import numpy as np

    def blocks(w, rows, cols):
        return [w[r * P:(r + 1) * P][:, c] for r, c in zip(rows, cols)]

    def cols(c):
        return slice(c, c + P)

    K8 = range(DT)
    units = []

    def unit(parts):
        u = np.zeros((P, UNIT), np.float32)
        at = 0
        for b in parts:
            u[:, at:at + b.shape[1]] = b
            at += b.shape[1]
        units.append(u)

    def column(w, c, rows=K8):
        return [w[r * P:(r + 1) * P][:, c] for r in rows]

    kr = np.r_[320:384, 384:416, 400:416, 384:400]
    for l in range(L1):
        w = inp["w_in"][l]
        unit(column(w, cols(0))), unit(column(w, cols(P))), unit(column(w, cols(256))), unit(column(w, kr))
        for c in range(416, 1952, P):
            unit(column(w, cols(c)))
        w = inp["w_uq"][l]
        for q in range(2):
            unit([b for h in range(4 * q, 4 * q + 4) for b in column(w, h * QK + np.r_[0:96, 80:96, 64:80], range(2))])
        unit([inp["w_ukv"][l]])
        for m in range(DT):
            c = cols(m * P)
            unit(column(inp["w_br_a"][l], c, range(4)) + column(inp["w_br_b"][l], c, range(2)))
            unit(column(inp["w_br_c"][l], c, range(2)) + column(inp["w_br_d"][l], c, range(2)))
            for b in range(4):
                unit(column(inp["w_in"][l], cols(1952 + b * D + m * P)))
        for m in range(DT):
            unit(column(inp["w_out"][l], cols(m * P)))
        t = 0
        for size in CHUNKS:
            for j in range(t, t + size):
                unit(column(inp["w_ffn_gate"][l], cols(j * P))), unit(column(inp["w_ffn_up"][l], cols(j * P)))
            for m in range(DT):
                unit(column(inp["w_ffn_down"][l], cols(m * P), range(t, t + size)))
            t += size
    w = inp["a_w_in_2"][0]
    for m in list(range(8, 16)) + list(range(8)):
        unit(column(w, cols(m * P)))
    for q in range(2):
        unit([inp["a_w_gate_2"][0, n] for n in range(4 * q, 4 * q + 4)])
    for m in range(DT):
        unit(column(inp["a_w_out_2"][0], cols(m * P)))

    def mlp(l):
        for q in range(QUARTERS):
            for j in range(8):
                unit(column(inp["w_up_2"][l], cols((8 * q + j) * P)))
            for m in range(DT):
                unit(column(inp["w_down_2"][l], cols(m * P), range(8 * q, 8 * q + 8)))
    mlp(0)
    for m in range(DT):
        unit(column(inp["w_kv_2"], cols(m * P)))
    for half in range(2):
        for q in range(4):
            unit(column(inp["w_kv_2"], slice(D + half * S, D + (half + 1) * S), range(2 * q, 2 * q + 2)))
    for m in range(DT):
        unit(column(inp["b_w_q_2"][0], cols(m * P)))
    for m in range(DT):
        unit(column(inp["b_w_o_2"][0], cols(m * P)))
    mlp(1)
    assert len(units) == NU

    vecs = np.zeros((P, NV), np.float32)

    def put(name, x):
        x = np.asarray(x).reshape(-1, P).T
        vecs[:, VCOL[name]:VCOL[name] + x.shape[1]] = x
    for l in range(L1):
        for n, k in (("pre_mix", "g_pre_mix"), ("cq", "g_cq"), ("ckv", "g_ckv"), ("pool_scale", "pool_scale"),
                     ("conv", "conv_w"), ("post_mix", "g_post_mix"), ("pre_ffn", "g_pre_ffn"), ("post_ffn", "g_post_ffn")):
            put(f"{n}{l}", inp[k][l])
        put(f"mlp{l}", inp["mlp_norm_2"][l])
    for n, k in (("a_norm", "a_norm_2"), ("a_conv", "a_conv_w_2"), ("a_conv_b", "a_conv_b_2"), ("a_bg", "a_b_gate_2"),
                 ("a_lam", "a_lambda_2"), ("kv_norm", "kv_norm_2"), ("b_norm", "b_norm_2")):
        put(n, inp[k])
    put("k_norm", np.tile(inp["k_norm_2"], 2)), put("q_norm", np.tile(inp["b_q_norm_2"][0], 2))
    vecs[0:64, VCOL["inv_win"]:VCOL["inv_win"] + 2] = (1 / 2, 1 / 8)
    vecs[64:128, VCOL["inv_win"]:VCOL["inv_win"] + 2] = (1 / 4, 1 / 16)
    vecs[:, VCOL["eps"]] = EPS

    inv = np.float32(10000.0) ** (-np.arange(0, ROPE, 2, dtype=np.float32) / np.float32(ROPE))
    ang = np.arange(S, dtype=np.float32)[:, None] * inv[None, :]
    cos, sin = np.cos(ang).T, np.sin(ang).T
    cossin = np.concatenate([np.ones((64, S), np.float32), cos, cos, -sin, sin]).astype(np.float32)
    fix = np.zeros((P, 2, 16), np.float32)
    for half in range(2):
        for t in range(2):
            win = (2, 4, 8, 16)[2 * t + half]
            fix[64 * half:64 * half + 64, t] = win / np.minimum(np.arange(16) + 1, win)
    pool_w = inp["pool_w"].reshape(L1, 2, P, 64).transpose(0, 2, 1, 3)
    sgu_wT = inp["sgu_w"].transpose(0, 3, 1, 2)
    sgu_b = np.repeat(inp["sgu_b"].reshape(L1, 2, 2, P), 64, axis=2).transpose(0, 2, 1, 3)
    sgu_g = np.repeat(inp["g_sgu_v"][:, None, :], P, axis=1)
    dist = np.arange(P)[:, None] + P - np.arange(2 * P)[None, :]
    bias2 = inp["b_rel_bias_2"][0][:, np.clip(dist, -63, 128) + 63].transpose(1, 0, 2)
    return {"xT": inp["x"][0].T, "w_all": np.stack(units), "vecs": vecs, "cossin": cossin, "win_fix": fix, "pool_w": pool_w,
            "sgu_wT": sgu_wT, "sgu_b": sgu_b, "sgu_g": sgu_g, "bias2": bias2}


def kernel(**inputs):
    import numpy as np
    import concourse.bacc as bacc
    from concourse.bass_utils import run_bass_kernel_spmd

    arrays = {k: np.ascontiguousarray(a) for k, a in lay_out({k: np.asarray(a) for k, a in inputs.items()}).items()}
    nc = bacc.Bacc("TRN2", target_bir_lowering=False, num_devices=1)
    args = [nc.dram_tensor(k, a.shape, F32, kind="ExternalInput").ap() for k, a in arrays.items()]
    out = nc.dram_tensor("outT", (D, S), F32, kind="ExternalOutput").ap()
    build(nc, *args, out)
    r = run_bass_kernel_spmd(nc, [arrays], core_ids=[0])
    return np.ascontiguousarray(r.results[0]["outT"].T)[None]
```

```python
import concourse.bass as bass
from concourse import mybir
from contextlib import ExitStack

F32 = mybir.dt.float32
F32R = mybir.dt.float32r
ALU = mybir.AluOpType
ACT = mybir.ActivationFunctionType
AX = mybir.AxisListType

P = 128
S = 512
D = 1024
DT = D // P
SCORE_AT = ((1, 384), (2, 0), (1, 0), (0, 0))
POOL_BANK = (4, 5, 6, 4)
EPS = 1e-6
NEG = -1e30
UNIT = 8 * P
WSLOTS = 4
RSLOTS = 2
AHEAD = 3

L1 = 2
H1, NOPE, ROPE, VH = 8, 64, 32, 64
QK = NOPE + ROPE
FT = 22
CHUNKS = (8, 8, 6)
U_IN, U_QKV, U_MERGE, U_OUT = 16, 3, 6 * DT, DT
U_FFN = 2 * FT + DT * len(CHUNKS)
U_LAYER = U_IN + U_QKV + U_MERGE + U_OUT + U_FFN
H2, HD2 = 16, 64
QUARTERS = 4
U_AIN, U_AGATE, U_AOUT = 16, 2, DT
U_MLP = QUARTERS * 2 * DT
U_K, U_V, U_Q, U_O = DT, 8, DT, DT
U_SECOND = U_AIN + U_AGATE + U_AOUT + U_MLP + U_K + U_V + U_Q + U_O + U_MLP
NU = L1 * U_LAYER + U_SECOND
B2 = L1 * U_LAYER

_names = []
for _l in range(L1):
    _names += [(f"pre_mix{_l}", 8), (f"cq{_l}", 2), (f"ckv{_l}", 1), (f"pool_scale{_l}", 2), (f"conv{_l}", 6),
               (f"post_mix{_l}", 8), (f"pre_ffn{_l}", 8), (f"post_ffn{_l}", 8)]
_names += [("a_norm", 8), ("a_conv", 32), ("a_conv_b", 8), ("a_bg", 16), ("a_lam", 8), ("kv_norm", 8),
           ("k_norm", 1), ("b_norm", 8), ("q_norm", 1), ("mlp0", 8), ("mlp1", 8), ("inv_win", 2), ("eps", 1)]
VCOL, NV = {}, 0
for _n, _k in _names:
    VCOL[_n] = NV
    NV += _k

NORMS = {}
_base, _pbase = 0, 0
for _n, _t, _pe in [x for l in range(L1) for x in ((f"pre_mix{l}", 8, l > 0), (f"cq{l}", 2, False), (f"ckv{l}", 1, False),
                                                  (f"post_mix{l}", 8, False), (f"pre_ffn{l}", 8, True),
                                                  (f"post_ffn{l}", 8, False))] + [
        ("a_norm", 8, True), ("mlp0", 8, False), ("kv_norm", 8, False), ("mlp1", 8, False)]:
    NORMS[_n] = (len(NORMS), _base, _pbase, _t, _pe)
    if _pe:
        _pbase += _t
    else:
        _base += _t
SPLIT, SRC, _at, _src = {}, {}, 0, 0
for _n, _t, _v in [x for l in range(L1) for x in ((f"pre_mix{l}", 8, 0), (f"cq{l}", 2, 0), (f"ckv{l}", 1, 1), (f"pool{l}", 2, 0),
                                                 (f"sgu{l}", 2, 1), (f"conv{l}", 2, 1), (f"att{l}", H1, 0),
                                                 (f"pre_ffn{l}", 8, 0), (f"ffn{l}", FT, 1))] + [
        ("a_norm", 8, 0), ("rec", 8, 1), ("lru", 8, 1), ("mlp_in0", 8, 0), ("mlp0", 32, 1), ("kv_norm", 8, 0),
        ("b_norm", 8, 0), ("att2", H2, 0), ("mlp_in1", 8, 0), ("mlp1", 32, 1)]:
    SPLIT[_n], SRC[_n] = _at, _src
    _at += _t
    _src += _t * _v
XDONE = {"post_mix0": 0, "post_ffn0": 8, "post_mix1": 16, "post_ffn1": 24, "a_out": 32, "mlp0": 40, "b_out": 48, "mlp1": 56}


def build(nc, xT, w_all, vecs, cossin, win_fix, pool_w, sgu_wT, sgu_b, sgu_g, bias2, outT):
    base = (nc.sbuf_base + 31) // 32 * 32
    place = [base]

    def at(name, shape, dt, offset):
        return nc.alloc_sbuf_tensor_at(name, shape, dt, offset=offset)

    def room(nbytes):
        o = place[0]
        place[0] += (nbytes + 31) // 32 * 32
        assert place[0] <= nc.sbuf_usable_end, place[0]
        return o
    KB = 1024
    X = at("X", [P, DT, S], F32, room(16 * KB))
    w_raw = at("w_raw", [P, RSLOTS, UNIT], F32, room(RSLOTS * 4 * KB))
    w_hi = at("w_hi", [P, WSLOTS, UNIT], F32R, room(WSLOTS * 4 * KB))
    w_lo = at("w_lo", [P, WSLOTS, UNIT], F32R, room(WSLOTS * 4 * KB))
    oh = room(32 * KB)
    H_hi = at("H_hi", [P, DT, S], F32R, oh)
    H_lo = at("H_lo", [P, DT, S], F32R, oh + 16 * KB)
    rel_bias = at("rel_bias", [P, H2, 2 * P], F32, oh)
    o1 = room(32 * KB)
    A = at("A", [P, 16, S], F32, o1)
    Q1 = at("Q1", [P, DT, S], F32, o1)
    K1 = at("K1", [P, DT, S], F32, o1 + 16 * KB)
    M_hi = at("M_hi", [P, DT, S], F32R, o1)
    M_lo = at("M_lo", [P, DT, S], F32R, o1 + 16 * KB)
    gelu_g = at("gelu_g", [P, DT, S], F32, o1)
    rec = at("rec", [P, DT, S], F32, o1 + 16 * KB)
    oy = room(40 * KB)
    Y_hi = at("Y_hi", [P, 10, S], F32R, oy)
    Y_lo = at("Y_lo", [P, 10, S], F32R, oy + 20 * KB)
    lru_r = at("lru_r", [P, DT, S], F32, oy)
    lru_i = at("lru_i", [P, DT, S], F32, oy + 20 * KB)
    o3 = room(25 * KB)
    V1 = at("V1", [P, 4, S], F32, o3)
    probs = at("probs", [P, 2, 1280], F32, o3 + 8 * KB)
    probsT = at("probsT", [P, 1280], F32, o3 + 18 * KB)
    C_hi = at("C_hi", [P, 3, S], F32R, o3)
    C_lo = at("C_lo", [P, 3, S], F32R, o3 + 6 * KB)
    Z = at("Z", [P, 2, 528], F32, o3 + 12 * KB)
    ZW = 4224
    SA = at("SA", [P, 2, 528], F32, o3 + 12 * KB + ZW)
    SB = at("SB", [P, 2, 528], F32, o3 + 12 * KB + 2 * ZW)
    gates = at("gates", [P, 4, S], F32, o3)
    ysb = at("ysb", [P, 4, S], F32, o3 + 8 * KB)
    tmp = at("tmp", [P, 2, S], F32, o3 + 16 * KB)
    Dn = at("Dn", [P, DT, S], F32, o3)
    recp = at("recp", [P, DT, 520], F32, o3)
    lru_t = at("lru_t", [P, DT, S], F32, o3)
    lru_u = at("lru_u", [P, S], F32, o3 + 20 * KB)
    fa = at("fa", [P, 2, S], F32, o3 + 16 * KB)
    fb = at("fb", [P, 2, S], F32, o3 + 20 * KB)
    V2 = at("V2", [P, 4, D], F32, o3)
    probs2 = at("probs2", [P, 2, 1280], F32, oh + 16 * KB)
    probsT2 = at("probsT2", [P, 1280], F32, oh + 26 * KB)
    RS2 = at("RS2", [P, S], F32, room(2 * KB))
    RS = at("RS", [P, S], F32, room(2 * KB))
    ACC = at("ACC", [P, S], F32, room(2 * KB))
    SQ = at("SQ", [P, 2, S], F32, room(4 * KB))
    XS = at("XS", [P, 2, S], F32, room(4 * KB))
    V = at("V", [P, NV], F32, room(NV * 4))
    CS = at("CS", [P, S], F32, room(2 * KB))
    ident = at("ident", [P, P], F32, room(512))
    ones = at("ones", [P, P], F32, room(512))
    ones64 = at("ones64", [P, P], F32, room(512))
    sel_row = at("sel_row", [1, P], F32, room(512))
    neg_row = at("neg_row", [1, 64], F32, room(256))
    winfix = at("winfix", [P, 2, 16], F32, room(128))
    poolw = at("poolw", [P, 2, 64], F32, room(512))
    sguw = at("sguw", [P, 4, P], F32, oy)
    sgub = at("sgub", [P, 2, P], F32, oy + 2 * KB)
    sgug = at("sgug", [P, 256], F32, oy + 3 * KB)
    st = at("st", [P, 2, 16], F32, room(128))
    sp = at("sp", [P, 40], F32, room(160))
    vnT = at("vnT", [P, 4, 256], F32, o3 + 12 * KB)

    ctx = ExitStack()
    with ctx:
        ps = ctx.enter_context(nc.psum_tensor("ps", [P, 8, S], F32))

        def sem(n):
            return ctx.enter_context(nc.semaphore(n))
        w_loaded = [sem(f"w_loaded{i}") for i in range(RSLOTS)]
        w_hi_ready, w_lo_ready, w_used, unit_out = sem("w_hi_ready"), sem("w_lo_ready"), sem("w_used"), sem("unit_out")
        consts_loaded, consts_made = sem("consts_loaded"), sem("consts_made")
        x_loaded = [sem(f"x_loaded{k}") for k in range(DT)]
        tables_loaded = sem("tables_loaded")
        layer_loaded = sem("layer_loaded")
        x_done = sem("x_done")
        sqp_ready, sq_summed = sem("sqp_ready"), sem("sq_summed")
        g_lin, rsT_sum, rsT_std = sem("g_lin"), sem("rsT_sum"), sem("rsT_std")
        gelu_in, cq_root = sem("gelu_in"), sem("cq_root")
        sq_ready, sq_added, ssum_ready, std_ready = sem("sq_ready"), sem("sq_added"), sem("ssum_ready"), sem("std_ready")
        src_ready = sem("src_ready")
        hi_ready = sem("hi_ready")
        lo_ready = sem("lo_ready")
        chain = sem("chain")
        a_chain = sem("a_chain")
        kr_ready, kr_spread = sem("kr_ready"), sem("kr_spread")
        qk_mm, qk_out = sem("qk_mm"), sem("qk_out")
        br_mm, br_act, br_vec = sem("br_mm"), sem("br_act"), sem("br_vec")
        s_ready, max_ready, exp_done, s_free = sem("s_ready"), sem("max_ready"), sem("exp_done"), sem("s_free")
        p_ready, t_done, pt_a, pt_v, pv_done = sem("p_ready"), sem("t_done"), sem("pt_a"), sem("pt_v"), sem("pv_done")
        sig_done, merged_lo = sem("sig_done"), sem("merged_lo")
        f_lin, f_act = sem("f_lin"), sem("f_act")
        lru_act, lru_vec = sem("lru_act"), sem("lru_vec")
        hn_sq, hn_mm, hn_std, hn_done = sem("hn_sq"), sem("hn_mm"), sem("hn_std"), sem("hn_done")
        bias_loaded = sem("bias_loaded")
        stored = sem("stored")

        def v(name, k=0, n=1):
            return V[:, VCOL[name] + k:VCOL[name] + k + n]

        def f(ap):
            return ap.bitcast(F32)

        def score(j, lo, hi):
            bank, c = SCORE_AT[j]
            return ps[:, bank, c + lo:c + hi]

        def first_units(l):
            u = l * U_LAYER
            return dict(win=u, qkv=u + U_IN, merge=u + U_IN + U_QKV, out=u + U_IN + U_QKV + U_MERGE,
                        ffn=u + U_IN + U_QKV + U_MERGE + U_OUT)

        UG = B2 + DT
        UGE = UG + U_AGATE
        UAO = UGE + DT
        UM0 = UAO + U_AOUT
        UK = UM0 + U_MLP
        UVV = UK + U_K
        UQ = UVV + U_V
        UO = UQ + U_Q
        UM1 = UO + U_O

        block = ctx.enter_context(nc.Block())

        @block.sync
        def _(eng):
            eng.dma_start(V[:], vecs).then_inc(consts_loaded, 16)
            eng.dma_start(w_raw[:, 0, :], w_all[0]).then_inc(w_loaded[0], 16)
            for k in range(DT):
                eng.dma_start(X[:, k, :], xT[k * P:(k + 1) * P, :]).then_inc(x_loaded[k], 16)
            eng.dma_start(w_raw[:, 1, :], w_all[1]).then_inc(w_loaded[1], 16)
            eng.dma_start(CS[:], cossin).then_inc(tables_loaded, 16)
            eng.dma_start(winfix[:], win_fix).then_inc(tables_loaded, 16)
            with eng.Fori(1, NU // RSLOTS) as i:
                for s in range(RSLOTS):
                    eng.wait_ge(w_lo_ready, i * RSLOTS + (s - RSLOTS + 1))
                    eng.dma_start(w_raw[:, s, :], w_all[bass.ds(i * RSLOTS + s, 1)].rearrange("o p n -> (o p) n")).then_inc(w_loaded[s], 16)
            for k in range(DT):
                eng.wait_ge(x_done, XDONE["mlp1"] + k + 1)
                eng.dma_start(outT[k * P:(k + 1) * P, :], X[:, k, :]).then_inc(stored, 16)
            eng.wait_ge(stored, 16 * DT)

        @block.gpsimd
        def _(eng):
            made = [0]

            def make(ins):
                made[0] += 1
                ins.then_inc(consts_made, 1)
                eng.wait_ge(consts_made, made[0])
            make(eng.memset(ident[:], 0.0))
            make(eng.affine_select(out=ident[:], in_=ident[:], compare_op=ALU.not_equal, fill=1.0, base=0,
                                   pattern=[[-1, P]], channel_multiplier=1))
            make(eng.memset(ones[:], 1.0))
            make(eng.memset(ones64[:], 0.0))
            make(eng.memset(ones64[0:64, 0:64], 1.0))
            make(eng.memset(ones64[64:128, 64:128], 1.0))
            make(eng.memset(sel_row[:], 0.0))
            make(eng.memset(sel_row[0:1, 0:64], 1.0))
            make(eng.memset(neg_row[:], NEG))
            with eng.Fori(0, NU // WSLOTS) as i:
                for s in range(WSLOTS):
                    eng.wait_ge(w_hi_ready, i * WSLOTS + (s + 1))
                    nc.gpsimd.tensor_tensor(w_lo[:, s, :], w_raw[:, s % RSLOTS, :], f(w_hi[:, s, :]),
                                            ALU.subtract).then_inc(w_lo_ready, 1)

        @block.scalar
        def _(act):
            def split_weights(u, c):
                if isinstance(u, int) and u >= NU:
                    return
                act.wait_ge(w_loaded[c % RSLOTS], (u - (c % RSLOTS)) * (16 // RSLOTS) + 16)
                if not isinstance(u, int) or u >= WSLOTS:
                    act.wait_ge(w_used, u + (1 - WSLOTS))
                nc.scalar.activation(w_hi[:, c % WSLOTS, :], w_raw[:, c % RSLOTS, :], ACT.Copy).then_inc(w_hi_ready, 1)

            def tick(u, c=None):
                split_weights(u + AHEAD, (u if c is None else c) + AHEAD)

            def norm(name, src, ready, d, split=None, dst=None, meanwhile=None):
                n, b, pb, t, on_pe = NORMS[name]
                for k in range(t):
                    if ready is x_loaded:
                        act.wait_ge(x_loaded[k], 16)
                    else:
                        act.wait_ge(ready[0], ready[1] + k + 1)
                    if on_pe:
                        if k >= 2:
                            act.wait_ge(sq_summed, pb // 8 * 7 + k - 1)
                        nc.scalar.activation(SQ[:, k % 2, :], src(k), ACT.Square).then_inc(sqp_ready, 1)
                    else:
                        if b + k >= 2:
                            act.wait_ge(sq_added, b + k - 1)
                        nc.scalar.activation(SQ[:, (b + k) % 2, :], src(k), ACT.Square).then_inc(sq_ready, 1)
                    if split:
                        nc.scalar.activation(dst(k), src(k), ACT.Copy, scale=v(name, k)).then_inc(hi_ready, 1)
                if meanwhile:
                    meanwhile()
                act.wait_ge(ssum_ready, n + 1)
                if not on_pe:
                    act.wait_ge(sq_added, b + t)
                nc.scalar.activation(SQ[:, 0 if on_pe else (b + t) % 2, :], ps[:, 7, :], ACT.Sqrt, bias=v("eps"), scale=1.0 / d).then_inc(std_ready, 1)

            H_dst = lambda k: H_hi[:, k, :]

            def split_src(name, t, dst, src):
                for k in range(t):
                    act.wait_ge(src_ready, SRC[name] + k + 1)
                    nc.scalar.activation(dst(k), src(k), ACT.Copy).then_inc(hi_ready, 1)

            def xs(name):
                return lambda k: XS[:, k % 2, :]

            def attention(g0, heads, split, second):
                def out_hi(g):
                    h = g - g0
                    r = slice(64 * (h % 2), 64 * (h % 2) + 64)
                    act.wait_ge(pv_done, g + 1)
                    nc.scalar.activation(Y_hi[r, h // 2, :], ps[r, 3 + 4 * (h % 2), :], ACT.Copy).then_inc(hi_ready, 1)

                def exps(g):
                    h = g - g0
                    act.wait_ge(max_ready, g + 1)
                    if g >= 2 and not second:
                        act.wait_ge(t_done, g - 1)
                    off = 0
                    for j in range(4):
                        w = P * (j + 1)
                        o = (probs2 if second else probs)[:, g % 2, off:off + w]
                        if second:
                            i = nc.scalar.activation(o, o, ACT.Exp, bias=st[:, g % 2, j:j + 1], scale=1.0, accum_out=st[:, g % 2, 4 + j:5 + j])
                        else:
                            i = nc.scalar.activation(o, score(j, 0, w), ACT.Exp, bias=st[:, g % 2, j:j + 1],
                                                     scale=QK ** -0.5, accum_out=st[:, g % 2, 4 + j:5 + j])
                        off += w
                    i.then_inc(exp_done, 1)
                prT = probsT2 if second else probsT
                exps(g0)
                for g in range(g0, g0 + heads):
                    act.wait_ge(t_done, g + 1)
                    if g:
                        act.wait_ge(pv_done, g)
                    nc.scalar.activation(prT[:, 0:S], ps[:, 4, :], ACT.Copy)
                    nc.scalar.activation(prT[:, S:S + 384], ps[:, 5, 0:384], ACT.Copy).then_inc(pt_a, 1)
                    if g > g0:
                        out_hi(g - 1)
                    if g + 1 < g0 + heads:
                        exps(g + 1)
                out_hi(g0 + heads - 1)

            act.wait_ge(consts_loaded, 16)
            for l in range(L1):
                U = first_units(l)
                if l:
                    act.wait_ge(w_used, U["win"])
                    act.wait_ge(lo_ready, SPLIT[f"conv{l - 1}"] + 2)
                for dst, src in ((poolw, pool_w), (sguw, sgu_wT), (sgub, sgu_b), (sgug, sgu_g)):
                    act.dma_start(dst[:], src[l]).then_inc(layer_loaded, 16)
                ready = x_loaded if l == 0 else (x_done, XDONE[f"post_ffn{l - 1}"])
                if l == 0:
                    split_weights(0, 0)
                norm(f"pre_mix{l}", lambda k: X[:, k, :], ready, D, True, H_dst, (lambda: [split_weights(u, u) for u in range(1, AHEAD)]) if l == 0 else None)
                w0 = U["win"]
                for u in range(w0, w0 + 4):
                    tick(u)
                norm(f"cq{l}", lambda k: A[:, k, :], (unit_out, w0), 256, True, lambda k: C_hi[:, k, :])
                tick(w0 + 4)
                act.wait_ge(cq_root, l + 1)
                norm(f"ckv{l}", lambda k: A[:, 2 + k, :], (unit_out, w0 + 2), 128)
                split_src(f"ckv{l}", 1, lambda k: C_hi[:, 2, :], xs(0))
                for u in range(w0 + 5, w0 + 10):
                    tick(u)
                act.wait_ge(br_mm, 3 * l + 1)
                for t in range(2):
                    for q in range(2):
                        r = slice(64 * q, 64 * q + 64)
                        i = nc.scalar.activation(Y_hi[r, 4 + t, :], ps[r, POOL_BANK[2 * t + q], :], ACT.Copy,
                                                 scale=V[r, VCOL[f"pool_scale{l}"] + t:VCOL[f"pool_scale{l}"] + t + 1])
                    i.then_inc(hi_ready, 1)
                tick(w0 + 10)
                act.wait_ge(br_mm, 3 * l + 2)
                for n in range(4):
                    nc.scalar.activation(SQ[:, 0, 0:256], ps[:, 5 + n // 2, (n % 2) * 256:(n % 2) * 256 + 256], ACT.Square,
                                         accum_out=st[:, 0, 8 + n:9 + n]).then_inc(a_chain, 1)
                    act.wait_ge(a_chain, 5 * l + n + 1)
                nc.scalar.activation(st[:, 1, 8:12], st[:, 0, 8:12], ACT.Sqrt, bias=v("eps"), scale=1.0 / 256).then_inc(a_chain, 1)
                act.wait_ge(a_chain, 5 * l + 5)
                for u in range(w0 + 11, w0 + 14):
                    tick(u)
                for k in range(2):
                    act.wait_ge(src_ready, SRC[f"sgu{l}"] + k + 1)
                    nc.scalar.activation(Y_hi[:, 6 + k, :], XS[:, k, :], ACT.Copy).then_inc(hi_ready, 1)
                for u in range(w0 + 14, w0 + U_IN):
                    tick(u)
                for k in range(2):
                    act.wait_ge(src_ready, SRC[f"conv{l}"] + k + 1)
                    nc.scalar.activation(Y_hi[:, 8 + k, :], XS[:, k, :], ACT.Copy).then_inc(hi_ready, 1)
                for u in range(U["qkv"], U["qkv"] + U_QKV):
                    tick(u)
                act.wait_ge(kr_ready, l + 1)
                for h in range(H1):
                    i = nc.scalar.activation(K1[64:96, h, :], tmp[64:96, 0, :], ACT.Copy)
                i.then_inc(kr_spread, 1)
                attention(l * H1, H1, f"att{l}", False)
                with act.Fori(0, DT // 2) as i:
                    for j in range(12):
                        c = U["merge"] + j
                        u = i * 12 + c
                        tick(u, c)
                        if j % 6 >= 2:
                            b = j % 6 - 2
                            act.wait_ge(g_lin, i * 8 + (l * 32 + 4 * (j // 6) + b + 1))
                            nc.scalar.activation(gates[:, b, :], gates[:, b, :], ACT.Sigmoid).then_inc(sig_done, 1)
                for u in range(U["out"], U["out"] + U_OUT):
                    tick(u)
                norm(f"post_mix{l}", lambda k: Dn[:, k, :], (unit_out, U["out"]), D)
                norm(f"pre_ffn{l}", lambda k: X[:, k, :], (x_done, XDONE[f"post_mix{l}"]), D, True, H_dst)

                def ffn(size, off, u0, i):
                    for j in range(size):
                        e = off + j + l * FT
                        for q in range(2):
                            tick(u0 + 2 * j + q if i is None else i * 24 + (u0 + 2 * j + q), u0 + 2 * j + q)
                        e = e if i is None else i * 8 + e
                        act.wait_ge(f_lin, e + 1)
                        nc.scalar.activation(fb[:, j % 2, :], fa[:, j % 2, :], ACT.Silu).then_inc(f_act, 1)
                        act.wait_ge(src_ready, e + (1 + SRC[f"ffn{l}"] - l * FT))
                        nc.scalar.activation(Y_hi[:, j, :], XS[:, j % 2, :], ACT.Copy).then_inc(hi_ready, 1)
                    for m in range(DT):
                        tick(u0 + 2 * size + m if i is None else i * 24 + (u0 + 2 * size + m), u0 + 2 * size + m)
                with act.Fori(0, 2) as i:
                    ffn(8, 0, U["ffn"], i)
                ffn(6, 16, U["ffn"] + 48, None)
                norm(f"post_ffn{l}", lambda k: Dn[:, k, :], (unit_out, U["ffn"] + U_FFN - 8), D)
            norm("a_norm", lambda k: X[:, k, :], (x_done, XDONE["post_ffn1"]), D, True, H_dst)
            act.wait_ge(lru_vec, 1)
            nc.scalar.activation(sp[:, 8:16], sp[:, 0:8], ACT.Exp).then_inc(lru_act, 1)
            act.wait_ge(lru_act, 1)
            nc.scalar.activation(sp[:, 16:24], sp[:, 8:16], ACT.Ln, bias=1.0).then_inc(lru_act, 1)
            for k in range(8):
                tick(B2 + k)
                act.wait_ge(src_ready, SRC["rec"] + k + 1)
                nc.scalar.activation(Y_hi[:, k, :], rec[:, k, :], ACT.Copy).then_inc(hi_ready, 1)
            for u in (UG, UG + 1):
                tick(u)
                act.wait_ge(w_used, u + 1)
                for q in range(4):
                    n = 4 * (u - UG) + q
                    nc.scalar.activation(lru_r[:, n, :], ps[:, 2 * q, :], ACT.Sigmoid, bias=v("a_bg", 2 * n))
                    nc.scalar.activation(lru_i[:, n, :], ps[:, 2 * q + 1, :], ACT.Sigmoid, bias=v("a_bg", 2 * n + 1)).then_inc(lru_act, 1)
            act.wait_ge(lru_act, 10)
            act.wait_ge(lru_vec, 2)
            for n in range(8):
                nc.scalar.activation(lru_t[:, n, :], lru_r[:, n, :], ACT.Tanh, scale=sp[:, 32 + n:33 + n]).then_inc(lru_act, 1)
            act.wait_ge(lru_act, 18)
            for n in range(8):
                nc.scalar.activation(lru_r[:, n, :], lru_r[:, n, :], ACT.Exp, scale=sp[:, 24 + n:25 + n]).then_inc(lru_act, 1)
            for n in range(8):
                tick(UGE + n)
                act.wait_ge(lru_vec, 3 + n)
                nc.scalar.activation(lru_t[:, n, :], lru_t[:, n, :], ACT.Sqrt).then_inc(lru_act, 1)
            for n in range(8):
                act.wait_ge(gelu_in, n + 1)
                nc.scalar.activation(gelu_g[:, n, :], gelu_g[:, n, :], ACT.Gelu_apprx_tanh).then_inc(lru_act, 1)
            for k in range(8):
                act.wait_ge(src_ready, SRC["lru"] + k + 1)
                nc.scalar.activation(Y_hi[:, k, :], XS[:, k % 2, :], ACT.Copy).then_inc(hi_ready, 1)
            for u in range(UAO, UAO + 8):
                tick(u)

            def mlp(n, U0):
                norm(f"mlp{n}", lambda k: X[:, k, :], (x_done, XDONE["a_out" if n == 0 else "b_out"]), D, True, H_dst)
                def quarter(i):
                    for j in range(8):
                        u = i * 16 + (U0 + j)
                        tick(u, U0 + j)
                        act.wait_ge(w_used, u + 1)
                        nc.scalar.activation(fa[:, j % 2, :], ps[:, (U0 + j) % 4, :], ACT.Relu).then_inc(f_act, 1)
                        act.wait_ge(src_ready, i * 8 + (SRC[f"mlp{n}"] + j + 1))
                        nc.scalar.activation(Y_hi[:, j, :], XS[:, j % 2, :], ACT.Copy).then_inc(hi_ready, 1)
                    for m in range(8):
                        tick(i * 16 + (U0 + 8 + m), U0 + 8 + m)
                with act.Fori(0, QUARTERS - 1) as i:
                    quarter(i)
                quarter(QUARTERS - 1)

            mlp(0, UM0)
            norm("kv_norm", lambda k: X[:, k, :], (x_done, XDONE["mlp0"]), D, True, H_dst)
            act.wait_ge(rsT_sum, 1)
            nc.scalar.activation(st[:, 1, 8:12], ps[:, 7, 0:4], ACT.Sqrt, bias=v("eps"), scale=1.0 / D).then_inc(rsT_std, 1)

            def head_norms(u0, buf, base):
                for t in range(8):
                    tick(u0 + t)
                    act.wait_ge(unit_out, u0 + t + 1)
                    nc.scalar.activation(SQ[:, 0, :], buf[:, t, :], ACT.Square).then_inc(hn_sq, 1)
                    act.wait_ge(hn_mm, base + t + 1)
                    nc.scalar.activation(SQ[:, 1, :], ps[:, 7, :], ACT.Sqrt, bias=v("eps"), scale=1.0 / HD2).then_inc(hn_std, 1)
                    act.wait_ge(hn_done, base + t + 1)
            head_norms(UK, K1, 0)
            for u in range(UVV, UVV + 8):
                tick(u)
            act.wait_ge(w_used, UVV + 8)
            for k in range(8):
                nc.scalar.activation(H_hi[:, k, :], X[:, k, :], ACT.Copy, scale=v("b_norm", k)).then_inc(hi_ready, 1)
            head_norms(UQ, Q1, 8)
            act.wait_ge(w_used, UQ + 8)
            act.dma_start(rel_bias[:], bias2).then_inc(bias_loaded, 16)
            attention(2 * H1, H2, "att2", True)
            for u in range(UO, UO + 8):
                tick(u)
            mlp(1, UM1)

        @block.tensor
        def _(pe):
            MM = nc.tensor.matmul

            def three(out, wh, wl, xh, xl, start, stop):
                MM(out, wh, xh, start=start, stop=False)
                MM(out, wh, xl, start=False, stop=False)
                return MM(out, wl, xh, start=False, stop=stop)

            def unit(u, c, out, xh, xl, tiles, free, ready=None, squares=None, step=1, made=lo_ready):
                pe.wait_ge(w_lo_ready, u + 1)
                if free is not None:
                    pe.wait_ge(unit_out, free)
                s = c % WSLOTS
                for k in range(tiles):
                    if squares:
                        squares(k)
                    if ready is not None:
                        pe.wait_ge(made, ready + (step * (k + 1)))
                    m = three(out, w_hi[:, s, k * P:(k + 1) * P], w_lo[:, s, k * P:(k + 1) * P], xh(k), xl(k), k == 0, k == tiles - 1)
                m.then_inc(w_used, 1)

            Hh, Hl = (lambda k: H_hi[:, k, :]), (lambda k: H_lo[:, k, :])
            Yh, Yl = (lambda k: Y_hi[:, k, :]), (lambda k: Y_lo[:, k, :])
            Mh, Ml = (lambda k: M_hi[:, k, :]), (lambda k: M_lo[:, k, :])

            def gemm(u0, n, xh, xl, tiles=8):
                for u in range(u0, u0 + n):
                    unit(u, u, ps[:, u % 4, :], xh, xl, tiles, u - 3 if u >= 4 else None)

            def square_sum(name):
                n, b, pb, t, on_pe = NORMS[name]

                def one(k):
                    if k == 0:
                        pe.wait_ge(std_ready, n)
                    pe.wait_ge(sqp_ready, pb + k + 1)
                    MM(ps[:, 7, :], ones[:], SQ[:, k % 2, :], start=k == 0, stop=k == t - 1).then_inc(sq_summed if k < t - 1 else ssum_ready, 1)
                return one

            def norm(name):
                n, b, pb, t, on_pe = NORMS[name]
                if on_pe:
                    for k in range(t):
                        square_sum(name)(k)
                    return
                pe.wait_ge(sq_added, b + t)
                if n:
                    pe.wait_ge(std_ready, n)
                MM(ps[:, 7, :], ones[:], ACC[:], start=True, stop=True).then_inc(ssum_ready, 1)

            def attention(g0, heads, second):
                pb = [4, 5, 6, 6]
                col = [0, 0, 0, 256]
                Vt, pr, prT = (V2, probs2, probsT2) if second else (V1, probs, probsT)

                def scores(g):
                    h = g - g0
                    if g > g0:
                        pe.wait_ge(s_free if second else exp_done, g - g0 if second else g)
                    for j in range(4):
                        w = P * (j + 1)
                        r = slice(64 * (h % 2), 64 * (h % 2) + 64) if second else slice(0, QK)
                        t = h // 2 if second else h
                        MM(score(j, 0, w), Q1[r, t, j * P:(j + 1) * P], K1[r, t, 0:w], start=True, stop=False)
                        m = MM(score(j, w - 64, w), sel_row[0:1, :], neg_row[0:1, :], start=False, stop=True)
                    m.then_inc(s_ready, 1)
                def turn(g):
                    pe.wait_ge(p_ready, g + 1)
                    if g:
                        pe.wait_ge(pt_a, g)
                        pe.wait_ge(pt_v, g)
                    off = 0
                    for j in range(4):
                        for i in range(j + 1):
                            c0 = col[i] + (j - i) * P
                            m = nc.tensor.transpose(ps[:, pb[i], c0:c0 + P], pr[:, g % 2, off + i * P:off + (i + 1) * P], ident[:])
                        off += (j + 1) * P
                    m.then_inc(t_done, 1)

                def values(g):
                    h = g - g0
                    pe.wait_ge(pt_a, g + 1)
                    pe.wait_ge(pt_v, g + 1)
                    if h >= 2:
                        pe.wait_ge(lo_ready, SPLIT["att2" if second else f"att{g0 // H1}"] + h - 1)
                    r = slice(64 * (h % 2), 64 * (h % 2) + 64)
                    o = 0
                    for i in range(4):
                        n = S - i * P
                        m = MM(ps[r, 3 + 4 * (h % 2), i * P:S], Vt[:, i, h * 64:(h + 1) * 64], prT[:, o:o + n], start=i == 0, stop=i == 3)
                        o += n
                    m.then_inc(pv_done, 1)

                scores(g0)
                for g in range(g0, g0 + heads):
                    if g + 1 < g0 + heads:
                        scores(g + 1)
                    if g > g0:
                        values(g - 1)
                    turn(g)
                values(g0 + heads - 1)

            pe.wait_ge(consts_made, 9)
            for l in range(L1):
                U = first_units(l)
                w0 = U["win"]
                unit(w0, w0, ps[:, w0 % 4, :], Hh, Hl, 8, w0 - 3 if l else None, SPLIT[f"pre_mix{l}"], square_sum(f"pre_mix{l}") if l else None)
                if l == 0:
                    norm("pre_mix0")
                gemm(w0 + 1, 4, Hh, Hl)
                norm(f"cq{l}")
                gemm(w0 + 5, 2, Hh, Hl)
                norm(f"ckv{l}")
                gemm(w0 + 7, 3, Hh, Hl)
                pe.wait_ge(layer_loaded, 64 * (l + 1))
                pe.wait_ge(br_vec, 3 * l + 1)
                for g in range(4):
                    r = slice(64 * (g % 2), 64 * (g % 2) + 64)
                    m = MM(ps[r, POOL_BANK[g], :], poolw[r, g // 2, :], (SA, SB)[g % 2][r, g // 2, 16:528], start=True, stop=True)
                m.then_inc(br_mm, 1)
                gemm(w0 + 10, 1, Hh, Hl)
                pe.wait_ge(lo_ready, SPLIT[f"pool{l}"] + 2)
                pe.wait_ge(unit_out, w0 + 8)
                for n in range(4):
                    for t in range(2):
                        c0 = (n % 2) * 256 + t * P
                        m = nc.tensor.transpose(ps[:, 5 + n // 2, c0:c0 + P], A[:, 6 + t, n * P:(n + 1) * P], ident[:])
                m.then_inc(br_mm, 1)
                gemm(w0 + 11, 2, Hh, Hl)
                pe.wait_ge(br_vec, 3 * l + 3)
                for g in range(4):
                    r = slice(64 * (g % 2), 64 * (g % 2) + 64)
                    for n in range(4):
                        m = MM(ps[r, 5 + g // 2, n * P:(n + 1) * P], vnT[:, n, g * 64:(g + 1) * 64], sguw[:, g, :], start=True, stop=True)
                m.then_inc(br_mm, 1)
                gemm(w0 + 13, 3, Hh, Hl)
                uq = U["qkv"]
                pe.wait_ge(lo_ready, SPLIT[f"sgu{l}"] + 2)
                for q in range(2):
                    u = uq + q
                    pe.wait_ge(w_lo_ready, u + 1)
                    if q:
                        pe.wait_ge(qk_out, 20 * l + 4)
                    else:
                        pe.wait_ge(unit_out, u)
                    for b in range(4):
                        for k in range(2):
                            c0 = (2 * b + k) * P
                            m = three(ps[:, b, :], w_hi[:, u % 4, c0:c0 + P], w_lo[:, u % 4, c0:c0 + P], C_hi[:, k, :], C_lo[:, k, :], k == 0, k == 1)
                    m.then_inc(w_used, 1)
                u = uq + 2
                pe.wait_ge(w_lo_ready, u + 1)
                for h in range(8):
                    if h < 4:
                        pe.wait_ge(qk_out, 20 * l + 8)
                    c0 = h * P
                    m = three(ps[:, h, :], w_hi[:, u % 4, c0:c0 + P], w_lo[:, u % 4, c0:c0 + P], C_hi[:, 2, :], C_lo[:, 2, :], True, True)
                m.then_inc(qk_mm, 1)
                pe.wait_ge(qk_out, 20 * l + 12)
                wh = w_hi[:, u % 4, :].rearrange("p (h c) -> p h c", c=P)[:, :, 64:128]
                wl = w_lo[:, u % 4, :].rearrange("p (h c) -> p h c", c=P)[:, :, 64:128]
                for i in range(4):
                    o = ps[:, i, :].rearrange("p (h c) -> p h c", c=64)
                    t = slice(i * P, (i + 1) * P)
                    MM(o, C_hi[:, 2, t], wh, start=True, stop=False)
                    MM(o, C_hi[:, 2, t], wl, start=False, stop=False)
                    m = MM(o, C_lo[:, 2, t], wh, start=False, stop=True)
                m.then_inc(w_used, 1)
                pe.wait_ge(qk_out, 20 * (l + 1))
                pe.wait_ge(kr_spread, l + 1)
                attention(l * H1, H1, False)
                with pe.Fori(0, DT // 2) as i:
                    for j in range(12):
                        c = U["merge"] + j
                        u = i * 12 + c
                        s = c % 4
                        if j % 6 < 2:
                            pe.wait_ge(w_lo_ready, u + 1)
                            pe.wait_ge(unit_out, u - 3)
                            parts = ((5, 4, (4, 5)), (4, 0, (0, 1, 2, 3))) if j % 6 == 0 else ((6, 0, (6, 7)), (7, 2, (8, 9)))
                            for bank, w0, ks in parts:
                                for n, k in enumerate(ks):
                                    c0 = (w0 + n) * P
                                    if j == 0 and bank == 4:
                                        pe.wait_ge(lo_ready, SPLIT[f"att{l}"] + 2 * (k + 1))
                                    m = three(ps[:, bank, :], w_hi[:, s, c0:c0 + P], w_lo[:, s, c0:c0 + P], Y_hi[:, k, :], Y_lo[:, k, :], n == 0, n == len(ks) - 1)
                            m.then_inc(w_used, 1)
                        else:
                            unit(u, c, ps[:, c % 4, :], Hh, Hl, 8, u - 3)
                uo = U["out"]
                unit(uo, uo, ps[:, uo % 4, :], Mh, Ml, 8, uo - 3, DT * l, made=merged_lo)
                gemm(uo + 1, U_OUT - 1, Mh, Ml)
                norm(f"post_mix{l}")
                norm(f"pre_ffn{l}")
                pe.wait_ge(lo_ready, SPLIT[f"pre_ffn{l}"] + 8)

                def ffn(size, u0, i, e):
                    for j in range(2 * size):
                        u = u0 + j if i is None else i * 24 + (u0 + j)
                        unit(u, u0 + j, ps[:, (u0 + j) % 4, :], Hh, Hl, 8, u - 3)
                    for m in range(8):
                        c = u0 + 2 * size + m
                        u = c if i is None else i * 24 + c
                        unit(u, c, ps[:, c % 4, :], Yh, Yl, size, u - 3, (e if i is None else i * 8 + e) if m == 0 else None)
                with pe.Fori(0, 2) as i:
                    ffn(8, U["ffn"], i, SPLIT[f"ffn{l}"])
                ffn(6, U["ffn"] + 48, None, SPLIT[f"ffn{l}"] + 16)
                norm(f"post_ffn{l}")
            unit(B2, B2, ps[:, B2 % 4, :], Hh, Hl, 8, B2 - 3, SPLIT["a_norm"], square_sum("a_norm"))
            gemm(B2 + 1, DT - 1, Hh, Hl)
            for u in (UG, UG + 1):
                pe.wait_ge(w_lo_ready, u + 1)
                pe.wait_ge(unit_out, UG)
                if u > UG:
                    pe.wait_ge(lru_act, 6)
                else:
                    pe.wait_ge(std_ready, NORMS["a_norm"][0] + 1)
                for q in range(4):
                    n = 4 * (u - UG) + q
                    pe.wait_ge(lo_ready, SPLIT["rec"] + n + 1)
                    for e in range(2):
                        c0 = (2 * q + e) * P
                        m = three(ps[:, 2 * q + e, :], w_hi[:, u % 4, c0:c0 + P], w_lo[:, u % 4, c0:c0 + P], Y_hi[:, n, :], Y_lo[:, n, :], True, True)
                m.then_inc(w_used, 1)
            pe.wait_ge(unit_out, UGE)
            gemm(UGE, DT, Hh, Hl)
            unit(UAO, UAO, ps[:, UAO % 4, :], Yh, Yl, 8, UAO - 3, SPLIT["lru"])
            gemm(UAO + 1, DT - 1, Yh, Yl)

            def mlp(n, U0):
                norm(f"mlp{n}")
                with pe.Fori(0, QUARTERS) as i:
                    for j in range(8):
                        unit(i * 16 + (U0 + j), U0 + j, ps[:, (U0 + j) % 4, :], Hh, Hl, 8, i * 16 + (U0 + j - 3),
                             None if j else SPLIT[f"mlp_in{n}"])
                    for m in range(8):
                        c = U0 + 8 + m
                        unit(i * 16 + c, c, ps[:, c % 4, :], Yh, Yl, 8, i * 16 + (c - 3), None if m else i * 8 + SPLIT[f"mlp{n}"])
            mlp(0, UM0)
            norm("kv_norm")
            unit(UK, UK, ps[:, UK % 4, :], Hh, Hl, 8, UK - 3, SPLIT["kv_norm"])
            pe.wait_ge(std_ready, NORMS["kv_norm"][0] + 1)
            for j in range(4):
                m = MM(ps[:, 7, j:j + 1], ACC[:, j * P:(j + 1) * P], ones[:, 0:1], start=True, stop=True)
            m.then_inc(rsT_sum, 1)

            def head_norm(t):
                pe.wait_ge(hn_sq, t + 1)
                if t == 0:
                    pe.wait_ge(rsT_std, 1)
                MM(ps[:, 7, :], ones64[:], SQ[:, 0, :], start=True, stop=True).then_inc(hn_mm, 1)
            for u in range(UK + 1, UK + 8):
                unit(u, u, ps[:, u % 4, :], Hh, Hl, 8, u - 3)
                head_norm(u - UK - 1)
            head_norm(7)
            for half in range(2):
                for q in range(4):
                    u = UVV + 4 * half + q
                    pe.wait_ge(w_lo_ready, u + 1)
                    if q == 0:
                        pe.wait_ge(unit_out, u)
                    for k in range(2):
                        wh, wl = w_hi[:, u % 4, k * S:(k + 1) * S], w_lo[:, u % 4, k * S:(k + 1) * S]
                        for i in range(4):
                            t = slice(i * P, (i + 1) * P)
                            first, last = q == 0 and k == 0, q == 3 and k == 1
                            MM(ps[:, i, :], H_hi[:, 2 * q + k, t], wh, start=first, stop=False)
                            MM(ps[:, i, :], H_hi[:, 2 * q + k, t], wl, start=False, stop=False)
                            m = MM(ps[:, i, :], H_lo[:, 2 * q + k, t], wh, start=False, stop=last)
                    m.then_inc(w_used, 1)
            pe.wait_ge(unit_out, UQ)
            for u in range(UQ, UQ + 8):
                unit(u, u, ps[:, u % 4, :], Hh, Hl, 8, u - 3, SPLIT["b_norm"] if u == UQ else None)
                if u > UQ:
                    head_norm(8 + u - UQ - 1)
            head_norm(15)
            pe.wait_ge(hn_done, 16)
            attention(2 * H1, H2, True)
            unit(UO, UO, ps[:, UO % 4, :], Yh, Yl, 8, UO - 3, SPLIT["att2"], step=2)
            gemm(UO + 1, DT - 1, Yh, Yl)
            mlp(1, UM1)

        @block.vector
        def _(dve):
            VE = nc.vector
            links = [0]

            def link(ins):
                links[0] += 1
                ins.then_inc(chain, 1)
                dve.wait_ge(chain, links[0])

            def looped(n, per, body):
                base = links[0]
                with dve.Fori(0, n) as i:
                    k = [0]

                    def lk(ins):
                        k[0] += 1
                        ins.then_inc(chain, 1)
                        dve.wait_ge(chain, i * per + (base + k[0]))
                    body(i, lk)
                assert k[0] == per, (k[0], per)
                links[0] = base + n * per

            def out_of(u):
                dve.sem_inc(unit_out, 1)

            def add_squares(name, k):
                n, b, pb, t, on_pe = NORMS[name]
                dve.wait_ge(sq_ready, b + k + 1)
                if k == 0:
                    i = VE.tensor_copy(ACC[:], SQ[:, (b + k) % 2, :])
                else:
                    i = VE.tensor_tensor(ACC[:], ACC[:], SQ[:, (b + k) % 2, :], ALU.add)
                i.then_inc(sq_added, 1)
                dve.wait_ge(sq_added, b + k + 1)

            def root(name, dst):
                n, b, pb, t, on_pe = NORMS[name]
                dve.wait_ge(std_ready, n + 1)
                return VE.reciprocal(dst, SQ[:, 0 if on_pe else (b + t) % 2, :])

            def lo_gain(split, k, src, gain, hi, lo):
                dve.wait_ge(hi_ready, SPLIT[split] + k + 1)
                VE.scalar_tensor_tensor(lo, src, gain, f(hi), ALU.mult, ALU.subtract).then_inc(lo_ready, 1)
                dve.wait_ge(lo_ready, SPLIT[split] + k + 1)

            def x_lo(split, gain, k):
                lo_gain(split, k, X[:, k, :], v(gain, k), H_hi[:, k, :], H_lo[:, k, :])

            def norm_x(name, split):
                for k in range(DT):
                    add_squares(name, k)
                    x_lo(split, name, k)
                link(root(name, RS[:]))

            def post_norm(name, then, split):
                for k in range(DT):
                    add_squares(name, k)
                link(root(name, RS[:]))
                for k in range(DT):
                    link(VE.scalar_tensor_tensor(XS[:, k % 2, :], Dn[:, k, :], v(name, k), RS[:], ALU.mult, ALU.mult))
                    VE.tensor_tensor(X[:, k, :], X[:, k, :], XS[:, k % 2, :], ALU.add).then_inc(x_done, 1)
                    dve.wait_ge(x_done, XDONE[name] + k + 1)
                    if k:
                        x_lo(split, then, k - 1)
                x_lo(split, then, DT - 1)
                link(root(then, RS[:]))

            def scaled_out(u, dst):
                dve.wait_ge(w_used, u + 1)
                VE.tensor_tensor(dst, ps[:, u % 4, :], RS[:], ALU.mult).then_inc(unit_out, 1)
                dve.wait_ge(unit_out, u + 1)

            def copy_out(u, dst):
                dve.wait_ge(w_used, u + 1)
                VE.tensor_copy(dst, ps[:, u % 4, :]).then_inc(unit_out, 1)
                dve.wait_ge(unit_out, u + 1)

            def attention(g0, heads, split, second):
                pr, prT = (probs2, probsT2) if second else (probs, probsT)

                def out_lo(h):
                    r = slice(64 * (h % 2), 64 * (h % 2) + 64)
                    lo_of(split, h, Y_lo[r, h // 2, :], ps[r, 3 + 4 * (h % 2), :], Y_hi[r, h // 2, :])

                def maxima(g):
                    h = g - g0
                    dve.wait_ge(s_ready, g + 1)
                    if second:
                        dve.wait_ge(t_done, g - 1)
                        off = 0
                        for j in range(4):
                            w = P * (j + 1)
                            far = max(0, w - 2 * P)
                            near = w - far
                            link(VE.scalar_tensor_tensor(pr[:, g % 2, off + far:off + w], score(j, far, w), HD2 ** -0.5,
                                                         rel_bias[:, h, 2 * P - near:2 * P], ALU.mult, ALU.add))
                            if far:
                                i = VE.tensor_scalar(pr[:, g % 2, off:off + far], score(j, 0, far), HD2 ** -0.5,
                                                     rel_bias[:, h, 0:1], ALU.mult, ALU.add)
                                link(i) if j < 3 else i.then_inc(s_free, 1)
                            off += w
                        dve.wait_ge(s_free, g - g0 + 1)
                        off = 0
                        for j in range(4):
                            w = P * (j + 1)
                            link(VE.tensor_reduce(st[:, g % 2, 8 + j:9 + j], pr[:, g % 2, off:off + w], AX.X, ALU.max))
                            off += w
                        VE.tensor_scalar(st[:, g % 2, 0:4], st[:, g % 2, 8:12], -1.0, None, ALU.mult).then_inc(max_ready, 1)
                    else:
                        for j in range(4):
                            link(VE.tensor_reduce(st[:, g % 2, 8 + j:9 + j], score(j, 0, P * (j + 1)), AX.X, ALU.max))
                        VE.tensor_scalar(st[:, g % 2, 0:4], st[:, g % 2, 8:12], -(QK ** -0.5), None, ALU.mult).then_inc(max_ready, 1)
                    dve.wait_ge(max_ready, g + 1)
                maxima(g0)
                for g in range(g0, g0 + heads):
                    h = g - g0
                    dve.wait_ge(exp_done, g + 1)
                    link(VE.reciprocal(st[:, g % 2, 12:16], st[:, g % 2, 4:8]))
                    off = 0
                    for j in range(4):
                        w = P * (j + 1)
                        o = pr[:, g % 2, off:off + w]
                        i = VE.tensor_scalar(o, o, st[:, g % 2, 12 + j:13 + j], None, ALU.mult)
                        if j < 3:
                            link(i)
                        off += w
                    i.then_inc(p_ready, 1)
                    dve.wait_ge(p_ready, g + 1)
                    if h + 1 < heads:
                        maxima(g + 1)
                    dve.wait_ge(t_done, g + 1)
                    if g:
                        dve.wait_ge(pv_done, g)
                    VE.tensor_copy(prT[:, S + 384:1280], ps[:, 6, 0:384]).then_inc(pt_v, 1)
                    dve.wait_ge(pt_v, g + 1)
                    if h:
                        out_lo(h - 1)
                out_lo(heads - 1)

            def lo_of(split, k, dst, src, hi):
                dve.wait_ge(hi_ready, SPLIT[split] + k + 1)
                VE.tensor_tensor(dst, src, f(hi), ALU.subtract).then_inc(lo_ready, 1)
                dve.wait_ge(lo_ready, SPLIT[split] + k + 1)

            dve.wait_ge(consts_loaded, 16)
            for l in range(L1):
                U = first_units(l)
                w0 = U["win"]

                def take(*units):
                    for j in units:
                        scaled_out(w0 + j, A[:, j, :])
                if l == 0:
                    norm_x("pre_mix0", "pre_mix0")
                take(0, 1, 2, 3)
                for k in range(2):
                    add_squares(f"cq{l}", k)
                    lo_gain(f"cq{l}", k, A[:, k, :], v(f"cq{l}", k), C_hi[:, k, :], C_lo[:, k, :])
                take(4)
                root(f"cq{l}", RS2[:]).then_inc(cq_root, 1)
                dve.wait_ge(cq_root, l + 1)
                add_squares(f"ckv{l}", 0)
                if l == 0:
                    dve.wait_ge(tables_loaded, 32)
                link(VE.tensor_tensor(RS2[:], RS2[:], CS[:], ALU.mult))
                take(5, 6)
                link(root(f"ckv{l}", XS[:, 1, :]))
                VE.scalar_tensor_tensor(XS[:, 0, :], A[:, 2, :], v(f"ckv{l}"), XS[:, 1, :], ALU.mult, ALU.mult).then_inc(src_ready, 1)
                dve.wait_ge(src_ready, SRC[f"ckv{l}"] + 1)
                lo_of(f"ckv{l}", 0, C_lo[:, 2, :], XS[:, 0, :], C_hi[:, 2, :])
                take(7)
                link(VE.memset(Z[:, :, 0:16], 0.0))
                link(VE.tensor_copy(Z[:, :, 16:528], A[:, 4:6, :]))
                link(VE.tensor_tensor(SA[:, :, 1:528], Z[:, :, 1:528], Z[:, :, 0:527], ALU.add))
                link(VE.tensor_tensor(SB[:, :, 3:528], SA[:, :, 3:528], SA[:, :, 1:526], ALU.add))
                link(VE.tensor_tensor(SA[:, 1, 7:528], SB[:, 1, 7:528], SB[:, 1, 3:524], ALU.add))
                link(VE.tensor_tensor(SB[64:128, 1, 15:528], SA[64:128, 1, 15:528], SA[64:128, 1, 7:520], ALU.add))
                for q, W in ((0, SA), (1, SB)):
                    r = slice(64 * q, 64 * q + 64)
                    link(VE.tensor_tensor(W[r, :, 16:32], W[r, :, 16:32], winfix[r, :, :], ALU.mult))
                    for t in range(2):
                        link(VE.scalar_tensor_tensor(W[r, t, 16:528], W[r, t, 16:528], V[r, VCOL["inv_win"] + t:VCOL["inv_win"] + t + 1],
                                                     A[r, 4 + t, :], ALU.mult, ALU.subtract))
                dve.sem_inc(br_vec, 1)
                take(8, 9)
                dve.wait_ge(layer_loaded, 64 * (l + 1))
                VE.memset(sguw[64:128, :, 0:64], 0.0).then_inc(br_vec, 1)
                dve.wait_ge(br_vec, 3 * l + 2)
                for t in range(2):
                    dve.wait_ge(hi_ready, SPLIT[f"pool{l}"] + t + 1)
                    for q in range(2):
                        r = slice(64 * q, 64 * q + 64)
                        i = VE.scalar_tensor_tensor(Y_lo[r, 4 + t, :], ps[r, POOL_BANK[2 * t + q], :], V[r, VCOL[f"pool_scale{l}"] + t:VCOL[f"pool_scale{l}"] + t + 1],
                                                    f(Y_hi[r, 4 + t, :]), ALU.mult, ALU.subtract)
                        if q == 0:
                            link(i)
                    i.then_inc(lo_ready, 1)
                    dve.wait_ge(lo_ready, SPLIT[f"pool{l}"] + t + 1)
                take(10, 11)
                dve.wait_ge(a_chain, 5 * l + 5)
                link(VE.reciprocal(st[:, 0, 12:16], st[:, 1, 8:12]))
                for n in range(4):
                    i = VE.scalar_tensor_tensor(vnT[:, n, :], ps[:, 5 + n // 2, (n % 2) * 256:(n % 2) * 256 + 256], st[:, 0, 12 + n:13 + n],
                                                sgug[:], ALU.mult, ALU.mult)
                    if n < 3:
                        link(i)
                i.then_inc(br_vec, 1)
                dve.wait_ge(br_vec, 3 * l + 3)
                take(12)
                dve.wait_ge(br_mm, 3 * l + 3)
                for t in range(2):
                    pm = ps[:, 5 + t, :].rearrange("p (n i) -> p n i", i=P)
                    bb = sgub[:, t:t + 1, :].to_broadcast([P, 4, P])
                    link(VE.tensor_tensor(XS[:, t, :].rearrange("p (n i) -> p n i", i=P), pm, bb, ALU.add))
                    VE.tensor_tensor(XS[:, t, :], XS[:, t, :], A[:, 8 + t, :], ALU.mult).then_inc(src_ready, 1)
                    dve.wait_ge(src_ready, SRC[f"sgu{l}"] + t + 1)
                for t in range(2):
                    lo_of(f"sgu{l}", t, Y_lo[:, 6 + t, :], XS[:, t, :], Y_hi[:, 6 + t, :])
                take(13)
                link(VE.memset(Z[:, :, 0:2], 0.0))
                link(VE.tensor_tensor(Z[:, :, 2:514], A[:, 10:12, :], A[:, 12:14, :], ALU.mult))
                cw = VCOL[f"conv{l}"]
                for t in range(2):
                    link(VE.tensor_scalar(XS[:, t, :], Z[:, t, 2:514], V[:, cw + 4 + t:cw + 5 + t], None, ALU.mult))
                    link(VE.scalar_tensor_tensor(XS[:, t, :], Z[:, t, 1:513], V[:, cw + 2 + t:cw + 3 + t], XS[:, t, :], ALU.mult, ALU.add))
                    link(VE.scalar_tensor_tensor(XS[:, t, :], Z[:, t, 0:512], V[:, cw + t:cw + 1 + t], XS[:, t, :], ALU.mult, ALU.add))
                take(14, 15)
                for t in range(2):
                    VE.tensor_tensor(XS[:, t, :], XS[:, t, :], A[:, 14 + t, :], ALU.mult).then_inc(src_ready, 1)
                    dve.wait_ge(src_ready, SRC[f"conv{l}"] + t + 1)
                link(VE.tensor_tensor(tmp[64:96, 0, :], A[64:96, 3, :], CS[64:96, :], ALU.mult))
                link(VE.tensor_tensor(tmp[64:96, 1, :], A[96:128, 3, :], CS[96:128, :], ALU.mult))
                VE.tensor_tensor(tmp[64:96, 0, :], tmp[64:96, 0, :], tmp[64:96, 1, :], ALU.add).then_inc(kr_ready, 1)
                dve.wait_ge(kr_ready, l + 1)
                for t in range(2):
                    lo_of(f"conv{l}", t, Y_lo[:, 8 + t, :], XS[:, t, :], Y_hi[:, 8 + t, :])
                for q in range(2):
                    u = U["qkv"] + q
                    dve.wait_ge(w_used, u + 1)
                    for b in range(4):
                        h = 4 * q + b
                        link(VE.tensor_tensor(Q1[0:96, h, :], ps[0:96, b, :], RS2[0:96, :], ALU.mult))
                        link(VE.tensor_tensor(tmp[64:96, 1, :], ps[96:128, b, :], RS2[96:128, :], ALU.mult))
                        VE.tensor_tensor(Q1[64:96, h, :], Q1[64:96, h, :], tmp[64:96, 1, :], ALU.add).then_inc(qk_out, 1)
                        dve.wait_ge(qk_out, 20 * l + h + 1)
                    out_of(u)
                dve.wait_ge(qk_mm, l + 1)
                for h in range(8):
                    VE.tensor_copy(K1[0:64, h, :], ps[0:64, h, :]).then_inc(qk_out, 1)
                    dve.wait_ge(qk_out, 20 * l + 9 + h)
                dve.wait_ge(w_used, U["qkv"] + 3)
                for i_ in range(4):
                    VE.tensor_copy(V1[:, i_, :], ps[:, i_, :]).then_inc(qk_out, 1)
                    dve.wait_ge(qk_out, 20 * l + 17 + i_)
                out_of(U["qkv"] + 2)
                attention(l * H1, H1, f"att{l}", False)

                def merge(i, lk):
                    for m in range(2):
                        for y in range(2):
                            c = U["merge"] + 6 * m + y
                            dve.wait_ge(w_used, i * 12 + (c + 1))
                            lk(VE.tensor_scalar(ysb[:, 2 * y, :], ps[:, 4 + 2 * y, :], 1.0, None, ALU.mult))
                            VE.tensor_scalar(ysb[:, 2 * y + 1, :], ps[:, 5 + 2 * y, :], 1.0, None, ALU.mult).then_inc(unit_out, 1)
                            dve.wait_ge(unit_out, i * 12 + (c + 1))
                        def weigh(b):
                            dve.wait_ge(sig_done, i * 8 + (l * 32 + 4 * m + b + 1))
                            lk(VE.tensor_tensor(XS[:, 0, :] if b else tmp[:, m, :], gates[:, b, :], ysb[:, b, :], ALU.mult))
                            if b:
                                lk(VE.tensor_tensor(tmp[:, m, :], tmp[:, m, :], XS[:, 0, :], ALU.add))
                        for b in range(4):
                            dve.wait_ge(w_used, i * 12 + (U["merge"] + 6 * m + 2 + b + 1))
                            VE.tensor_tensor(gates[:, b, :], ps[:, (U["merge"] + 6 * m + 2 + b) % 4, :], RS[:], ALU.mult).then_inc(g_lin, 1)
                            dve.wait_ge(g_lin, i * 8 + (l * 32 + 4 * m + b + 1))
                            dve.sem_inc(unit_out, 1)
                            if b:
                                weigh(b - 1)
                        weigh(3)
                        lk(VE.tensor_scalar(M_hi[:, i * 2 + m, :], tmp[:, m, :], 1.0, None, ALU.mult))
                        VE.tensor_tensor(M_lo[:, i * 2 + m, :], tmp[:, m, :], f(M_hi[:, i * 2 + m, :]), ALU.subtract).then_inc(merged_lo, 1)
                        dve.wait_ge(merged_lo, i * 2 + (l * DT + m + 1))
                looped(DT // 2, 2 * 10, merge)
                for u in range(U["out"], U["out"] + U_OUT):
                    copy_out(u, Dn[:, u - U["out"], :])
                post_norm(f"post_mix{l}", f"pre_ffn{l}", f"pre_ffn{l}")
                def ffn(size, u0, i, off, lk):
                    st_ = 24
                    at_ = (lambda c: c) if i is None else (lambda c: i * st_ + c)
                    e_ = (lambda c: c) if i is None else (lambda c: i * 8 + c)
                    for j in range(size):
                        dve.wait_ge(w_used, at_(u0 + 2 * j + 1))
                        VE.tensor_tensor(fa[:, j % 2, :], ps[:, (u0 + 2 * j) % 4, :], RS[:], ALU.mult).then_inc(f_lin, 1)
                        dve.wait_ge(f_lin, e_(l * FT + off + j + 1))
                        dve.sem_inc(unit_out, 1)
                        dve.wait_ge(w_used, at_(u0 + 2 * j + 2))
                        dve.wait_ge(f_act, e_(l * FT + off + j + 1))
                        lk(VE.tensor_tensor(XS[:, j % 2, :], fb[:, j % 2, :], ps[:, (u0 + 2 * j + 1) % 4, :], ALU.mult))
                        dve.sem_inc(unit_out, 1)
                        VE.tensor_tensor(XS[:, j % 2, :], XS[:, j % 2, :], RS[:], ALU.mult).then_inc(src_ready, 1)
                        k0 = SPLIT[f"ffn{l}"] + off + j + 1
                        dve.wait_ge(src_ready, e_(SRC[f"ffn{l}"] + off + j + 1))
                        dve.wait_ge(hi_ready, e_(k0))
                        VE.tensor_tensor(Y_lo[:, j, :], XS[:, j % 2, :], f(Y_hi[:, j, :]), ALU.subtract).then_inc(lo_ready, 1)
                        dve.wait_ge(lo_ready, e_(k0))
                    for m in range(8):
                        c = u0 + 2 * size + m
                        dve.wait_ge(w_used, at_(c + 1))
                        VE.tensor_tensor(Dn[:, m, :], Dn[:, m, :], ps[:, c % 4, :], ALU.add).then_inc(unit_out, 1)
                        dve.wait_ge(unit_out, at_(c + 1))
                link(VE.memset(Dn[:], 0.0))
                looped(2, 8, lambda i, lk: ffn(8, U["ffn"], i, 0, lk))
                ffn(6, U["ffn"] + 48, None, 16, link)
                post_norm(f"post_ffn{l}", *(("a_norm", "a_norm") if l == L1 - 1 else (f"pre_mix{l + 1}", f"pre_mix{l + 1}")))
            link(VE.tensor_scalar(sp[:, 24:32], v("a_lam", 0, 8), -1.0, None, ALU.mult))
            link(VE.tensor_tensor(sp[:, 0:8], sp[:, 24:32], v("a_lam", 0, 8), ALU.min))
            VE.tensor_scalar(sp[:, 32:40], sp[:, 24:32], 0.0, None, ALU.max).then_inc(lru_vec, 1)
            dve.wait_ge(lru_vec, 1)
            link(VE.memset(recp[:, :, 0:3], 0.0))
            for k in range(8):
                u = B2 + k
                scaled_out(u, recp[:, k, 3:515])
                link(VE.tensor_scalar(rec[:, k, :], recp[:, k, 3:515], v("a_conv", 24 + k), v("a_conv_b", k), ALU.mult, ALU.add))
                for j in (2, 1):
                    link(VE.scalar_tensor_tensor(rec[:, k, :], recp[:, k, j:j + S], v("a_conv", 8 * j + k), rec[:, k, :], ALU.mult, ALU.add))
                VE.scalar_tensor_tensor(rec[:, k, :], recp[:, k, 0:S], v("a_conv", k), rec[:, k, :], ALU.mult, ALU.add).then_inc(src_ready, 1)
                dve.wait_ge(src_ready, SRC["rec"] + k + 1)
                lo_of("rec", k, Y_lo[:, k, :], rec[:, k, :], Y_hi[:, k, :])
            dve.wait_ge(lru_act, 2)
            link(VE.tensor_tensor(sp[:, 24:32], sp[:, 16:24], sp[:, 32:40], ALU.add))
            link(VE.tensor_scalar(sp[:, 32:40], sp[:, 24:32], 8.0, None, ALU.mult))
            VE.tensor_scalar(sp[:, 24:32], sp[:, 32:40], -1.0, None, ALU.mult).then_inc(lru_vec, 1)
            dve.wait_ge(lru_vec, 2)
            for q in range(2):
                dve.wait_ge(lru_act, 6 + 4 * q)
                dve.sem_inc(unit_out, 1)

            def recur(n):
                dve.wait_ge(lru_act, 27 + n)
                link(VE.tensor_tensor(lru_i[:, n, :], lru_i[:, n, :], lru_t[:, n, :], ALU.mult))
                link(VE.tensor_tensor_scan(lru_t[:, n, :], lru_r[:, n, :], lru_i[:, n, :], 0.0, ALU.mult, ALU.add))
            for n in range(8):
                u = UGE + n
                dve.wait_ge(w_used, u + 1)
                VE.tensor_tensor(gelu_g[:, n, :], ps[:, u % 4, :], RS[:], ALU.mult).then_inc(gelu_in, 1)
                dve.wait_ge(gelu_in, n + 1)
                dve.sem_inc(unit_out, 1)
                dve.wait_ge(lru_act, 19 + n)
                link(VE.tensor_tensor(lru_u[:], lru_r[:, n, :], lru_r[:, n, :], ALU.mult))
                VE.scalar_tensor_tensor(lru_t[:, n, :], lru_u[:], 1.0, lru_t[:, n, :], ALU.add, ALU.mult).then_inc(lru_vec, 1)
                dve.wait_ge(lru_vec, 3 + n)
                link(VE.tensor_tensor(lru_i[:, n, :], lru_i[:, n, :], rec[:, n, :], ALU.mult))
                if n:
                    recur(n - 1)
            recur(7)
            for n in range(8):
                dve.wait_ge(lru_act, 35 + n)
                VE.tensor_tensor(XS[:, n % 2, :], lru_t[:, n, :], gelu_g[:, n, :], ALU.mult).then_inc(src_ready, 1)
                dve.wait_ge(src_ready, SRC["lru"] + n + 1)
                if n:
                    lo_of("lru", n - 1, Y_lo[:, n - 1, :], XS[:, (n - 1) % 2, :], Y_hi[:, n - 1, :])
            lo_of("lru", 7, Y_lo[:, 7, :], XS[:, 1, :], Y_hi[:, 7, :])

            def add_to_x(u, k, name):
                dve.wait_ge(w_used, u + 1)
                VE.tensor_tensor(X[:, k, :], X[:, k, :], ps[:, u % 4, :], ALU.add).then_inc(x_done, 1)
                dve.wait_ge(x_done, XDONE[name] + k + 1)
                dve.sem_inc(unit_out, 1)
            for k in range(8):
                add_to_x(UAO + k, k, "a_out")

            def mlp(n, U0):
                norm_x(f"mlp{n}", f"mlp_in{n}")

                def ups(i, lk):
                    for j in range(8):
                        dve.wait_ge(f_act, i * 8 + (L1 * FT + n * 32 + j + 1))
                        dve.sem_inc(unit_out, 1)
                        k0 = SPLIT[f"mlp{n}"] + j + 1
                        lk(VE.tensor_tensor(fb[:, 0, :], fa[:, j % 2, :], RS[:], ALU.mult))
                        VE.tensor_tensor(XS[:, j % 2, :], fb[:, 0, :], fb[:, 0, :], ALU.mult).then_inc(src_ready, 1)
                        dve.wait_ge(src_ready, i * 8 + (SRC[f"mlp{n}"] + j + 1))
                        dve.wait_ge(hi_ready, i * 8 + k0)
                        VE.tensor_tensor(Y_lo[:, j, :], XS[:, j % 2, :], f(Y_hi[:, j, :]), ALU.subtract).then_inc(lo_ready, 1)
                        dve.wait_ge(lo_ready, i * 8 + k0)

                def body(i, lk):
                    ups(i, lk)
                    for m in range(8):
                        c = U0 + 8 + m
                        dve.wait_ge(w_used, i * 16 + (c + 1))
                        VE.tensor_tensor(X[:, m, :], X[:, m, :], ps[:, c % 4, :], ALU.add).then_inc(unit_out, 1)
                        dve.wait_ge(unit_out, i * 16 + (c + 1))
                looped(QUARTERS, 8, body)
                for k in range(8):
                    dve.sem_inc(x_done, 1)

            mlp(0, UM0)
            norm_x("kv_norm", "kv_norm")
            dve.wait_ge(rsT_std, 1)
            link(VE.reciprocal(st[:, 0, 8:12], st[:, 1, 8:12]))

            def head_norms(u0, buf, base, gain):
                for t in range(8):
                    scaled_out(u0 + t, buf[:, t, :])
                    dve.wait_ge(hn_std, base + t + 1)
                    link(VE.reciprocal(XS[:, 0, :], SQ[:, 1, :]))
                    VE.scalar_tensor_tensor(buf[:, t, :], buf[:, t, :], v(gain), XS[:, 0, :], ALU.mult, ALU.mult).then_inc(hn_done, 1)
                    dve.wait_ge(hn_done, base + t + 1)
            head_norms(UK, K1, 0, "k_norm")
            for half in range(2):
                for q in range(3):
                    dve.sem_inc(unit_out, 1)
                dve.wait_ge(w_used, UVV + 4 * half + 4)
                for i_ in range(4):
                    link(VE.tensor_scalar(V2[:, i_, half * S:(half + 1) * S], ps[:, i_, :], st[:, 0, 8 + i_:9 + i_], None, ALU.mult))
                dve.sem_inc(unit_out, 1)
            for k in range(8):
                x_lo("b_norm", "b_norm", k)
            head_norms(UQ, Q1, 8, "q_norm")
            dve.wait_ge(bias_loaded, 16)
            attention(2 * H1, H2, "att2", True)
            for k in range(8):
                add_to_x(UO + k, k, "b_out")
            mlp(1, UM1)


def lay_out(inp):
    import numpy as np

    def blocks(w, rows, cols):
        return [w[r * P:(r + 1) * P][:, c] for r, c in zip(rows, cols)]

    def cols(c):
        return slice(c, c + P)

    K8 = range(DT)
    units = []

    def unit(parts):
        u = np.zeros((P, UNIT), np.float32)
        at = 0
        for b in parts:
            u[:, at:at + b.shape[1]] = b
            at += b.shape[1]
        units.append(u)

    def column(w, c, rows=K8):
        return [w[r * P:(r + 1) * P][:, c] for r in rows]

    kr = np.r_[320:384, 384:416, 400:416, 384:400]
    for l in range(L1):
        w = inp["w_in"][l]
        unit(column(w, cols(0))), unit(column(w, cols(P))), unit(column(w, cols(256))), unit(column(w, kr))
        for c in [c0 + o for c0 in (416, 928, 672, 1440, 1696, 1184) for o in (0, P)]:
            unit(column(w, cols(c)))
        w = inp["w_uq"][l]
        for q in range(2):
            unit([b for h in range(4 * q, 4 * q + 4) for b in column(w, h * QK + np.r_[0:96, 80:96, 64:80], range(2))])
        unit([inp["w_ukv"][l]])
        for m in range(DT):
            c = cols(m * P)
            unit(column(inp["w_br_a"][l], c, range(4)) + column(inp["w_br_b"][l], c, range(2)))
            unit(column(inp["w_br_c"][l], c, range(2)) + column(inp["w_br_d"][l], c, range(2)))
            for b in range(4):
                unit(column(inp["w_in"][l], cols(1952 + b * D + m * P)))
        for m in range(DT):
            unit(column(inp["w_out"][l], cols(m * P)))
        t = 0
        for size in CHUNKS:
            for j in range(t, t + size):
                unit(column(inp["w_ffn_gate"][l], cols(j * P))), unit(column(inp["w_ffn_up"][l], cols(j * P)))
            for m in range(DT):
                unit(column(inp["w_ffn_down"][l], cols(m * P), range(t, t + size)))
            t += size
    w = inp["a_w_in_2"][0]
    for m in range(8, 16):
        unit(column(w, cols(m * P)))
    for q in range(2):
        unit([inp["a_w_gate_2"][0, n] for n in range(4 * q, 4 * q + 4)])
    for m in range(8):
        unit(column(w, cols(m * P)))
    for m in range(DT):
        unit(column(inp["a_w_out_2"][0], cols(m * P)))

    def mlp(l):
        for q in range(QUARTERS):
            for j in range(8):
                unit(column(inp["w_up_2"][l], cols((8 * q + j) * P)))
            for m in range(DT):
                unit(column(inp["w_down_2"][l], cols(m * P), range(8 * q, 8 * q + 8)))
    mlp(0)
    for m in range(DT):
        unit(column(inp["w_kv_2"], cols(m * P)))
    for half in range(2):
        for q in range(4):
            unit(column(inp["w_kv_2"], slice(D + half * S, D + (half + 1) * S), range(2 * q, 2 * q + 2)))
    for m in range(DT):
        unit(column(inp["b_w_q_2"][0], cols(m * P)))
    for m in range(DT):
        unit(column(inp["b_w_o_2"][0], cols(m * P)))
    mlp(1)
    assert len(units) == NU

    vecs = np.zeros((P, NV), np.float32)

    def put(name, x):
        x = np.asarray(x).reshape(-1, P).T
        vecs[:, VCOL[name]:VCOL[name] + x.shape[1]] = x
    for l in range(L1):
        for n, k in (("pre_mix", "g_pre_mix"), ("cq", "g_cq"), ("ckv", "g_ckv"), ("pool_scale", "pool_scale"),
                     ("conv", "conv_w"), ("post_mix", "g_post_mix"), ("pre_ffn", "g_pre_ffn"), ("post_ffn", "g_post_ffn")):
            put(f"{n}{l}", inp[k][l])
        put(f"mlp{l}", inp["mlp_norm_2"][l])
    for n, k in (("a_norm", "a_norm_2"), ("a_conv", "a_conv_w_2"), ("a_conv_b", "a_conv_b_2"), ("a_bg", "a_b_gate_2"),
                 ("a_lam", "a_lambda_2"), ("kv_norm", "kv_norm_2"), ("b_norm", "b_norm_2")):
        put(n, inp[k])
    put("k_norm", np.tile(inp["k_norm_2"], 2)), put("q_norm", np.tile(inp["b_q_norm_2"][0], 2))
    vecs[0:64, VCOL["inv_win"]:VCOL["inv_win"] + 2] = (1 / 2, 1 / 8)
    vecs[64:128, VCOL["inv_win"]:VCOL["inv_win"] + 2] = (1 / 4, 1 / 16)
    vecs[:, VCOL["eps"]] = EPS

    inv = np.float32(10000.0) ** (-np.arange(0, ROPE, 2, dtype=np.float32) / np.float32(ROPE))
    ang = np.arange(S, dtype=np.float32)[:, None] * inv[None, :]
    cos, sin = np.cos(ang).T, np.sin(ang).T
    cossin = np.concatenate([np.ones((64, S), np.float32), cos, cos, -sin, sin]).astype(np.float32)
    fix = np.zeros((P, 2, 16), np.float32)
    for half in range(2):
        for t in range(2):
            win = (2, 4, 8, 16)[2 * t + half]
            fix[64 * half:64 * half + 64, t] = win / np.minimum(np.arange(16) + 1, win)
    pool_w = inp["pool_w"].reshape(L1, 2, P, 64).transpose(0, 2, 1, 3)
    sgu_wT = inp["sgu_w"].transpose(0, 3, 1, 2)
    sgu_b = np.repeat(inp["sgu_b"].reshape(L1, 2, 2, P), 64, axis=2).transpose(0, 2, 1, 3)
    sgu_g = np.repeat(inp["g_sgu_v"][:, None, :], P, axis=1)
    dist = np.arange(P)[:, None] + P - np.arange(2 * P)[None, :]
    bias2 = inp["b_rel_bias_2"][0][:, np.clip(dist, -63, 128) + 63].transpose(1, 0, 2)
    return {"xT": inp["x"][0].T, "w_all": np.stack(units), "vecs": vecs, "cossin": cossin, "win_fix": fix, "pool_w": pool_w,
            "sgu_wT": sgu_wT, "sgu_b": sgu_b, "sgu_g": sgu_g, "bias2": bias2}


def kernel(**inputs):
    import numpy as np
    import concourse.bacc as bacc
    from concourse.bass_utils import run_bass_kernel_spmd

    arrays = {k: np.ascontiguousarray(a) for k, a in lay_out({k: np.asarray(a) for k, a in inputs.items()}).items()}
    nc = bacc.Bacc("TRN2", target_bir_lowering=False, num_devices=1)
    args = [nc.dram_tensor(k, a.shape, F32, kind="ExternalInput").ap() for k, a in arrays.items()]
    out = nc.dram_tensor("outT", (D, S), F32, kind="ExternalOutput").ap()
    build(nc, *args, out)
    r = run_bass_kernel_spmd(nc, [arrays], core_ids=[0])
    return np.ascontiguousarray(r.results[0]["outT"].T)[None]
```
